# Optimizing a Trainium2 kernel written in Bass

```python
import jax, jax.numpy as jnp
from jax import lax
import numpy as np

D_MODEL = 2048
BATCH = 1
SEQ = 512
DEPTH = 1

CHUNK = 64
Q_BLOCK = 128
HEAD_DIM = 128
N_FOX_HEADS = D_MODEL // (2 * HEAD_DIM)
N_RET_HEADS = D_MODEL // (2 * HEAD_DIM)
D_FOX = N_FOX_HEADS * HEAD_DIM
D_RET = N_RET_HEADS * HEAD_DIM
D_MIX = D_FOX + D_RET
D_IN = 3 * D_FOX + N_FOX_HEADS + 4 * D_RET
N_GROUPS = 4
EXPERTS_PER_GROUP = 8
N_EXPERTS = N_GROUPS * EXPERTS_PER_GROUP
TOP_K = 2
D_EXPERT = D_MODEL // 4
MOE_BLOCK = 128
ROPE_BASE = 10000.0
EPS = 1e-6
FORGET_BIAS_INIT = 3.0

kernel_name = "hybrid_fox_retention_hmoe_adaln"

def rms_norm(x, w):
    xf = x.astype(jnp.float32)
    y = xf * lax.rsqrt(jnp.mean(xf * xf, axis=-1, keepdims=True) + EPS)
    return (y * w.astype(jnp.float32)).astype(x.dtype)

def rotate(x, pos):
    half = HEAD_DIM // 2
    theta = ROPE_BASE ** (-jnp.arange(half, dtype=jnp.float32) / half)
    ang = pos[:, None] * theta[None, :]
    cos = jnp.cos(ang)[None, :, None, :]
    sin = jnp.sin(ang)[None, :, None, :]
    x1, x2 = x[..., :half], x[..., half:]
    return jnp.concatenate([x1 * cos - x2 * sin, x1 * sin + x2 * cos], axis=-1).astype(x.dtype)

def forgetting_attention(q, k, v, log_f):
    B, H, S, d = q.shape
    nb = S // Q_BLOCK
    cum = jnp.cumsum(log_f, axis=-1)
    key_pos = jnp.arange(S)
    scale = HEAD_DIM ** -0.5
    qb = q.reshape(B, H, nb, Q_BLOCK, d).transpose(2, 0, 1, 3, 4)
    cb = cum.reshape(B, H, nb, Q_BLOCK).transpose(2, 0, 1, 3)

    def block(args):
        i, q_i, c_i = args
        s = jnp.einsum('bhqd,bhkd->bhqk', q_i, k).astype(jnp.float32) * scale
        s = s + c_i[..., :, None] - cum[..., None, :]
        q_pos = i * Q_BLOCK + jnp.arange(Q_BLOCK)
        s = jnp.where(key_pos[None, :] <= q_pos[:, None], s, -jnp.inf)
        p = jax.nn.softmax(s, axis=-1).astype(v.dtype)
        return jnp.einsum('bhqk,bhkd->bhqd', p, v)

    out = lax.map(block, (jnp.arange(nb), qb, cb))
    return out.transpose(1, 2, 0, 3, 4).reshape(B, H, S, d)

def retention(q, k, v):
    B, H, S, d = q.shape
    nc = S // CHUNK
    log_g = jnp.log(1.0 - 2.0 ** (-5.0 - jnp.arange(H, dtype=jnp.float32)))
    idx = jnp.arange(CHUNK, dtype=jnp.float32)
    diff = idx[:, None] - idx[None, :]
    decay = jnp.where(diff >= 0, jnp.exp(log_g[:, None, None] * jnp.maximum(diff, 0.0)), 0.0)
    q_decay = jnp.exp(log_g[:, None] * (idx + 1.0))
    k_decay = jnp.exp(log_g[:, None] * (CHUNK - 1.0 - idx))
    chunk_decay = jnp.exp(log_g * CHUNK)
    qc = q.reshape(B, H, nc, CHUNK, d)
    kc = k.reshape(B, H, nc, CHUNK, d) * (HEAD_DIM ** -0.5)
    vc = v.reshape(B, H, nc, CHUNK, d)
    scores = jnp.einsum('bhnid,bhnjd->bhnij', qc, kc) * decay[None, :, None]
    intra = jnp.einsum('bhnij,bhnje->bhnie', scores, vc)
    kv = jnp.einsum('bhnjd,bhnje->bhnde', kc * k_decay[None, :, None, :, None], vc)

    def step(state, kv_i):
        return state * chunk_decay[None, :, None, None] + kv_i, state

    _, prev = lax.scan(step, jnp.zeros((B, H, d, d), kv.dtype), kv.transpose(2, 0, 1, 3, 4))
    prev = prev.transpose(1, 2, 0, 3, 4)
    inter = jnp.einsum('bhnid,bhnde->bhnie', qc * q_decay[None, :, None, :, None], prev)
    return (intra + inter).reshape(B, H, S, d).astype(v.dtype)

def hierarchical_moe(h, w_coarse, b_coarse, w_fine, b_fine, w1, w3, w2):
    N, D = h.shape
    hf = h.astype(jnp.float32)
    p_group = jax.nn.softmax(hf @ w_coarse.astype(jnp.float32) + b_coarse.astype(jnp.float32), axis=-1)
    g_sel = jnp.argmax(p_group, axis=-1)
    p_g = jnp.take_along_axis(p_group, g_sel[:, None], axis=-1)
    fine_all = jnp.einsum('nd,gde->nge', hf, w_fine.astype(jnp.float32)) + b_fine.astype(jnp.float32)
    fine = jnp.take_along_axis(fine_all, g_sel[:, None, None], axis=1)[:, 0]
    top_p, top_e = lax.top_k(jax.nn.softmax(fine, axis=-1), TOP_K)
    gate = p_g * top_p / jnp.sum(top_p, axis=-1, keepdims=True)
    eid = g_sel[:, None] * EXPERTS_PER_GROUP + top_e
    NK = N * TOP_K
    flat_e = eid.reshape(NK).astype(jnp.int32)
    flat_w = gate.reshape(NK)
    flat_tok = jnp.repeat(jnp.arange(N, dtype=jnp.int32), TOP_K)
    order = jnp.argsort(flat_e)
    e_s, tok_s, w_s = flat_e[order], flat_tok[order], flat_w[order]
    counts = jnp.zeros((N_EXPERTS,), jnp.int32).at[flat_e].add(1)
    padded = (counts + MOE_BLOCK - 1) // MOE_BLOCK * MOE_BLOCK
    start = jnp.cumsum(counts) - counts
    pstart = jnp.cumsum(padded) - padded
    pend = pstart + padded
    dest = pstart[e_s] + (jnp.arange(NK, dtype=jnp.int32) - start[e_s])
    nb = NK // MOE_BLOCK + N_EXPERTS
    slot_tok = jnp.full((nb * MOE_BLOCK,), N, jnp.int32).at[dest].set(tok_s)
    slot_w = jnp.zeros((nb * MOE_BLOCK,), h.dtype).at[dest].set(w_s.astype(h.dtype))
    block_start = jnp.arange(nb, dtype=jnp.int32) * MOE_BLOCK
    block_e = jnp.minimum(jnp.searchsorted(pend, block_start, side='right'), N_EXPERTS - 1)
    xpad = jnp.concatenate([h, jnp.zeros((1, D), h.dtype)], axis=0)
    xb = xpad[slot_tok].reshape(nb, MOE_BLOCK, D)

    def expert_block(args):
        x_i, e = args
        return (jax.nn.silu(x_i @ w1[e]) * (x_i @ w3[e])) @ w2[e]

    yb = lax.map(expert_block, (xb, block_e))
    y = jnp.zeros((N + 1, D), yb.dtype).at[slot_tok].add(yb.reshape(-1, D) * slot_w[:, None])
    return y[:N]

def setup_inputs(seed: int = 0) -> dict:
    key = jax.random.key(seed)
    ks = jax.random.split(key, 20)
    L, D = DEPTH, D_MODEL
    nrm = jax.random.normal
    return {
        "x": nrm(ks[0], (BATCH, SEQ, D), jnp.float32),
        "c": nrm(ks[1], (BATCH, D), jnp.float32),
        "w_ada": nrm(ks[2], (L, D, 6 * D), jnp.float32) * D ** -0.5,
        "b_ada": 0.02 * nrm(ks[3], (L, 6 * D), jnp.float32),
        "norm1_w": 1.0 + 0.01 * nrm(ks[4], (L, D), jnp.float32),
        "w_in": nrm(ks[5], (L, D, D_IN), jnp.float32) * D ** -0.5,
        "forget_bias": FORGET_BIAS_INIT + 0.1 * nrm(ks[6], (L, N_FOX_HEADS), jnp.float32),
        "q_norm_w": 1.0 + 0.01 * nrm(ks[7], (L, HEAD_DIM), jnp.float32),
        "k_norm_w": 1.0 + 0.01 * nrm(ks[8], (L, HEAD_DIM), jnp.float32),
        "ret_norm_w": 1.0 + 0.01 * nrm(ks[9], (L, D_RET), jnp.float32),
        "w_out": nrm(ks[10], (L, D_MIX, D), jnp.float32) * D_MIX ** -0.5,
        "norm2_w": 1.0 + 0.01 * nrm(ks[11], (L, D), jnp.float32),
        "w_coarse": nrm(ks[12], (L, D, N_GROUPS), jnp.float32) * D ** -0.5,
        "b_coarse": 0.01 * nrm(ks[13], (L, N_GROUPS), jnp.float32),
        "w_fine": nrm(ks[14], (L, N_GROUPS, D, EXPERTS_PER_GROUP), jnp.float32) * D ** -0.5,
        "b_fine": 0.01 * nrm(ks[15], (L, N_GROUPS, EXPERTS_PER_GROUP), jnp.float32),
        "w1": nrm(ks[16], (L, N_EXPERTS, D, D_EXPERT), jnp.float32) * D ** -0.5,
        "w3": nrm(ks[17], (L, N_EXPERTS, D, D_EXPERT), jnp.float32) * D ** -0.5,
        "w2": nrm(ks[18], (L, N_EXPERTS, D_EXPERT, D), jnp.float32) * D_EXPERT ** -0.5,
    }

def reference(x, c, w_ada, b_ada, norm1_w, w_in, forget_bias, q_norm_w, k_norm_w, ret_norm_w,
              w_out, norm2_w, w_coarse, b_coarse, w_fine, b_fine, w1, w3, w2):
    B, S, D = x.shape
    H, d = N_FOX_HEADS, HEAD_DIM
    Hr = N_RET_HEADS
    splits = [D_FOX, 2 * D_FOX, 3 * D_FOX, 3 * D_FOX + H,
              3 * D_FOX + H + D_RET, 3 * D_FOX + H + 2 * D_RET, 3 * D_FOX + H + 3 * D_RET]
    pos = jnp.arange(S, dtype=jnp.float32)
    c_act = jax.nn.silu(c)
    for l in range(DEPTH):
        mod = c_act @ w_ada[l] + b_ada[l]
        sh1, sc1, g1, sh2, sc2, g2 = jnp.split(mod[:, None, :], 6, axis=-1)
        h = rms_norm(x, norm1_w[l]) * (1.0 + sc1) + sh1
        z = h @ w_in[l]
        qa, ka, va, fa, qb, kb, vb, gb = jnp.split(z, splits, axis=-1)
        qa = rms_norm(qa.reshape(B, S, H, d), q_norm_w[l]).transpose(0, 2, 1, 3)
        ka = rms_norm(ka.reshape(B, S, H, d), k_norm_w[l]).transpose(0, 2, 1, 3)
        va = va.reshape(B, S, H, d).transpose(0, 2, 1, 3)
        log_f = jax.nn.log_sigmoid(fa.astype(jnp.float32) + forget_bias[l].astype(jnp.float32))
        o_a = forgetting_attention(qa, ka, va, log_f.transpose(0, 2, 1))
        o_a = o_a.transpose(0, 2, 1, 3).reshape(B, S, D_FOX)
        qb = rotate(qb.reshape(B, S, Hr, d), pos).transpose(0, 2, 1, 3)
        kb = rotate(kb.reshape(B, S, Hr, d), pos).transpose(0, 2, 1, 3)
        vb = vb.reshape(B, S, Hr, d).transpose(0, 2, 1, 3)
        o_b = retention(qb, kb, vb).transpose(0, 2, 1, 3)
        o_b = rms_norm(o_b, ret_norm_w[l].reshape(Hr, d)).reshape(B, S, D_RET)
        o_b = o_b * jax.nn.silu(gb)
        mix = jnp.concatenate([o_a, o_b], axis=-1) @ w_out[l]
        x = x + g1 * mix
        h2 = rms_norm(x, norm2_w[l]) * (1.0 + sc2) + sh2
        y = hierarchical_moe(h2.reshape(B * S, D), w_coarse[l], b_coarse[l], w_fine[l], b_fine[l],
                             w1[l], w3[l], w2[l])
        x = x + g2 * y.reshape(B, S, D).astype(x.dtype)
    return x


_drawn_inputs = setup_inputs


def setup_inputs(seed=0):
    import zlib

    import numpy as np

    out = dict(_drawn_inputs(seed))
    spreads = {}
    factors = {'norm1_w': 4.779,
     'forget_bias': 2.883,
     'q_norm_w': 5.334,
     'k_norm_w': 4.419,
     'ret_norm_w': 3.284,
     'norm2_w': 2.886,
     'b_coarse': 3.705,
     'b_fine': 6.961}
    for name, (base, spread) in spreads.items():
        noise = np.random.default_rng([zlib.crc32(name.encode()), seed]).standard_normal(out[name].shape)
        drawn = base * np.exp(spread * noise) if base else spread * noise
        out[name] = __import__('jax').numpy.asarray(drawn.astype(out[name].dtype))
    for name, factor in factors.items():
        out[name] = (out[name] * factor).astype(out[name].dtype)
    return out
```

```python
from contextlib import ExitStack

import numpy as np

import concourse.bass as bass
from concourse import mybir
from concourse.alu_op_type import AluOpType as ALU

F32 = mybir.dt.float32
F32R = mybir.dt.float32r
I32 = mybir.dt.int32
U32 = mybir.dt.uint32
ACT = mybir.ActivationFunctionType
AX = mybir.AxisListType

P = 128
D = 2048
S = 512
HD = 128
NH = 8
KT = D // P
TT = S // P
COLS = 512
HG = COLS // HD
D_IN = 3 * 1024 + NH + 4 * 1024
NG, EPG = 4, 8
NE = NG * EPG
DE = 512
FT = DE // P
EPS = 1e-6
BIG = 1.0e30

FOX_CHUNKS, RET_CHUNKS, GROUPS = 3, 4, 2
FOX_COL = (1024, 0, 2048)
FORGET_COL = 3072
RET_COL = (3080, 4104, 5128, 6152)
WC = KT // 2
WRING = 4
FOX_W, RET_W = FOX_CHUNKS * WC, RET_CHUNKS * WC
Z_RET = GROUPS * FOX_CHUNKS
Z_OUT = Z_RET + GROUPS * RET_CHUNKS
N_OUT = D // COLS
ADA = 1024
ADA0_GROUPS = 2 * D // ADA
ADA0_RING = 4
ADA_GROUPS = 2
ADA_BODY = ADA_GROUPS * KT
UNITS = HG * TT

SLOTS = 64
MAX_ITEMS = NE + (2 * S - 1) // SLOTS + 1
ITEM_PIECES = 12
RAW = 6
SPL = 4
Y_AFTER, UV_AFTER, SILU_AFTER, A_AFTER = 1, 8, 9, 10
NOWHERE = 8191
TABLE = MAX_ITEMS + 2


def constants():
    half = HD // 2
    theta = np.float32(10000.0) ** (-np.arange(half, dtype=np.float32) / np.float32(half))
    ang = np.arange(S, dtype=np.float32)[:, None] * theta[None, :]
    rot = np.stack([np.cos(ang), np.sin(ang)], 1).astype(np.float32)
    rot = rot.reshape(TT, P, 2, half).transpose(1, 2, 0, 3)
    g = 1.0 - 2.0 ** (-5.0 - np.arange(NH))
    diff = np.arange(S)[None, :] - np.arange(P)[:, None]
    decay = np.where(diff >= 0, g[:, None, None] ** np.maximum(diff, 0)[None], 0.0) * HD ** -0.5
    upper = np.triu(np.ones((P, P), np.float32))
    pair = np.concatenate([np.eye(SLOTS), np.eye(SLOTS)]).astype(np.float32)
    one_head = np.zeros((NH, NH, P), np.float32)
    for h in range(NH):
        one_head[h, h] = 1.0
    iota = np.broadcast_to(np.arange(NE, dtype=np.float32), (P, NE))
    table = np.full((SLOTS, TABLE, 2), NOWHERE, np.int32)
    extra = MAX_ITEMS - NE
    which = np.zeros((1, extra, NE), np.float32) + np.arange(extra, dtype=np.float32)[None, :, None]
    twice = (2 * (np.arange(TT)[None, :] * P + np.arange(P)[:, None])).astype(np.float32)
    c = {
        "ident": np.eye(P, dtype=np.float32),
        "rot": np.ascontiguousarray(rot),
        "decay": decay.astype(np.float32),
        "causal": np.where(upper.T > 0, 0.0, -BIG).astype(np.float32),
        "strict": upper - np.eye(P, dtype=np.float32),
        "pair": pair,
        "one_head": one_head.reshape(NH, NH * P),
        "iota": np.ascontiguousarray(iota),
        "table0": table.reshape(SLOTS, -1),
        "which": which.reshape(1, -1),
        "twice": twice,
    }
    return {k: np.ascontiguousarray(v) for k, v in c.items()}


class Chain:

    def __init__(self, eng, sem, base):
        self.eng, self.sem, self.base, self.n = eng, sem, base, 0

    def __call__(self, ins):
        self.n += 1
        ins.then_inc(self.sem, 1)
        self.eng.wait_ge(self.sem, self.base + self.n)


def hybrid_block(nc, A, out):
    ctx = ExitStack()
    with ctx:
        size = 212832
        ctx.enter_context(nc.sbuf_tensor("arena", [P, size // 4], F32))
        origin = 16512

        def at(name, shape, dtype, offset):
            n = 4 * int(np.prod(shape[1:]))
            assert offset % 32 == 0 and offset + n <= size, (name, offset, n)
            return nc.alloc_sbuf_tensor_at(name, shape, dtype, offset=origin + offset)

        def dram(name, shape, dtype=F32):
            return nc.dram_tensor(name, shape, dtype, kind="Internal").ap()

        def sem(name):
            return ctx.enter_context(nc.semaphore(name))

        psum = ctx.enter_context(nc.psum_tensor("psum", [P, 8, 512], F32))

        w_raw = at("w_raw", [P, WRING, 2 * COLS], F32, 0)
        w_hi = at("w_hi", [P, WRING, 2 * COLS], F32R, 16384)
        w_lo = at("w_lo", [P, WRING, 2 * COLS], F32R, 32768)
        ada_raw = at("ada_raw", [P, 2, ADA], F32, 49152)
        ada_acc = at("ada_acc", [P, ADA], F32, 57344)
        act_hi = at("act_hi", [P, KT, S], F32R, 61440)
        act_lo = at("act_lo", [P, KT, S], F32R, 94208)
        act32 = at("act32", [P, KT, S], F32, 94208)
        square_out = at("square_out", [P, D], F32, 61440)
        C0 = 126976
        ident = at("ident", [P, P], F32, C0)
        rot_tab = at("rot_tab", [P, 2, TT, HD // 2], F32, C0 + 512)
        vec_cols = at("vec_cols", [P, P], F32, C0 + 2560)
        mod_cols = at("mod_cols", [P, 96], F32, C0 + 3072)
        head_cols = at("head_cols", [P, 10], F32, C0 + 3456)
        ones = at("ones", [P, 1], F32, C0 + 3520)
        c_cols = at("c_cols", [P, KT], F32, C0 + 3552)
        minus_half = at("minus_half", [P, KT], F32, C0 + 3616)
        ssq = at("ssq", [P, KT], F32, C0 + 3680)
        rstd = at("rstd", [P, KT], F32, C0 + 3744)
        row_max = at("row_max", [P, 2], F32, C0 + 3808)
        row_sum = at("row_sum", [P, 2], F32, C0 + 3840)
        row_inv = at("row_inv", [P, 2], F32, C0 + 3872)
        assert C0 + 3904 <= 130912
        B0 = 130912
        x1 = at("x1", [P, TT, D], F32, B0)
        zst = at("zst", [P, TT, COLS], F32, B0)
        qT = at("qT", [P, HG, S], F32, B0 + 8192)
        kT = at("kT", [P, HG, S], F32, B0 + 16384)
        v_sb = at("v_sb", [P, TT, COLS], F32, B0 + 24576)
        pT = at("pT", [P, HG, 10 * P], F32, B0 + 32768)
        probs = at("probs", [P, 2, S], F32, B0 + 53248)
        one_head = at("one_head", [NH, NH * P], F32, B0 + 57344)
        neg_cum = at("neg_cum", [NH, S], F32, B0 + 61440)
        head_sel = at("head_sel", [NH, HG * P], F32, B0 + 63488)
        causal = at("causal", [P, P], F32, B0 + 65536)
        f_raw = at("f_raw", [P, KT, NH], F32, B0 + 66048)
        f_hi = at("f_hi", [P, KT, NH], F32R, B0 + 66560)
        f_lo = at("f_lo", [P, KT, NH], F32R, B0 + 67072)
        f_bias = at("f_bias", [NH, 1], F32, B0 + 67584)
        f_y = at("f_y", [NH, S], F32, B0 + 69632)
        f_e = at("f_e", [NH, S], F32, B0 + 71680)
        f_ones = at("f_ones", [NH, S], F32, B0 + 73728)
        gate = at("gate", [P, TT, COLS], F32, B0 + 53248)
        rot = at("rot", [P, TT, HG, 2, HD // 2], F32, B0 + 61440)
        o_sb = at("o_sb", [P, HG, TT, HD], F32, B0 + 61440)
        decay = at("decay", [P, 2, S], F32, B0 + 69632)
        sq = at("sq", [P, COLS], F32, B0 + 75776)
        o_stage = at("o_stage", [P, 2, S], F32, B0 + 77824)
        o_back = at("o_back", [P, 10, S], F32, B0 + 32768)
        o_back2 = at("o_back2", [P, 2, S], F32, B0 + 77824)
        ret_out = at("ret_out", [P, HG, S], F32, B0 + 16384)
        ada0_raw = at("ada0_raw", [P, ADA0_RING, 2 * ADA], F32, B0)
        ada0_acc = at("ada0_acc", [P, 2, ADA], F32, B0 + 32768)
        x_st = at("x_st", [P, 2, D], F32, B0 + 49152)
        vec_rows = at("vec_rows", [P, P], F32, B0 + 69632)
        head_rows = at("head_rows", [10, P], F32, B0 + 70144)
        c_tmp = at("c_tmp", [P, KT], F32, B0 + 70656)
        g1_row = at("g1_row", [P, 2, COLS], F32, 49152)
        mod_rows_sb = at("mod_rows_sb", [64, P], F32, 57344)
        mix_tmp = at("mix_tmp", [P, COLS], F32, 53248 + 2048)
        ss2 = at("ss2", [P, TT, N_OUT], F32, 57856)
        sq2 = at("sq2", [P, COLS], F32, 58368)
        R0 = 163680
        m_raw = at("m_raw", [P, RAW, D], F32, R0)
        scale2 = at("scale2", [P, D], F32, R0 + 4 * 8192)
        shift2 = at("shift2", [P, D], F32, R0 + 5 * 8192)
        m_hi = at("m_hi", [P, SPL, D], F32R, 0)
        m_lo = at("m_lo", [P, SPL, D], F32R, 32768)
        pair = at("pair", [P, SLOTS], F32, 65536)
        table = at("table", [SLOTS, TABLE, 2], I32, 65792)
        idx_in = at("idx_in", [SLOTS, 1], I32, 66208)
        idx_out = at("idx_out", [SLOTS, 1], I32, 66240)
        gates = at("gates", [P, TT, 2], F32, 66272)
        extra_e = at("extra_e", [1, MAX_ITEMS - NE], I32, 66304)
        n_items = at("n_items", [1, 1], I32, 66368)
        xg = at("xg", [SLOTS, D], F32, 67584)
        xT = at("xT", [P, KT, 2, SLOTS], F32R, 75776)
        uv_sb = at("uv_sb", [P, 2, DE], F32, 83968)
        aT32 = at("aT32", [P, FT, SLOTS], F32, 88064)
        sig = at("sig", [P, FT, SLOTS], F32, 89088)
        aT = at("aT", [P, FT, 2, SLOTS], F32R, 90112)
        y_low = at("y_low", [SLOTS, D], F32, 92160)
        y_sb = at("y_sb", [SLOTS, D], F32, 100352)
        h2 = at("h2", [P, 2, D], F32, 92160)
        h2T = at("h2T", [P, KT, P], F32, 108544)
        route_w = at("route_w", [P, KT, NG + NE], F32, 116736)
        route_b = at("route_b", [P, NG + NE], F32, 119040)
        strict = at("strict", [P, P], F32, 119200)
        ones2 = at("ones2", [P, P], F32, 119712)
        iota = at("iota", [P, NE], F32, 120224)
        logit = at("logit", [P, TT, NG + NE], F32, 120352)
        coarse8 = at("coarse8", [P, 8], F32, 120928)
        top8 = at("top8", [P, 2, 8], F32, 120960)
        idx8 = at("idx8", [P, 2, 8], U32, 121024)
        pick = at("pick", [P, TT, 2], F32, 121088)
        hot = at("hot", [P, TT, 2, NE], F32, 121120)
        member = at("member", [P, TT, NE], F32, 122144)
        fine = at("fine", [P, NE], F32, 122656)
        small = at("small", [P, 16], F32, 122784)
        count = at("count", [P, NE], F32, 122848)
        count_i = at("count_i", [P, NE], I32, 122976)
        over = at("over", [P, NE], F32, 123104)
        over_end = at("over_end", [P, NE], F32, 123232)
        over_from = at("over_from", [P, NE], F32, 123360)
        wide = at("wide", [P, TT * 2, NE], F32, 123488)
        rank = at("rank", [P, TT, NE], F32, 124512)
        per = at("per", [P, 8, TT * 2], F32, 125024)
        per_i = at("per_i", [P, 2, TT * 2], I32, 125280)
        slot_i = at("slot_i", [P, TT * 2], I32, 125344)
        entry = at("entry", [P, TT * 2, 2], I32, 125376)
        twice = at("twice", [P, TT], F32, 125440)
        which = at("which", [1, (MAX_ITEMS - NE) * NE], F32, 98304 - 6144)
        which_o = at("which_o", [1, MAX_ITEMS - NE, NE], F32, 98304)
        extra_f = at("extra_f", [1, MAX_ITEMS - NE], F32, 125472)
        r_exp = at("r_exp", [P, KT + TT], F32, 125600)
        ms2 = at("ms2", [P, TT], F32, 125536)
        r2 = at("r2", [P, TT], F32, 125568)
        y_in = at("y_in", [P, 2, 2, D], F32, 0)
        g2_row = at("g2_row", [P, D], F32, 32768)
        fin = at("fin", [P, 2, D], F32, 40960)

        o_dram = dram("o_dram", [2 * NH, P, S])
        mod_dram = dram("mod_dram", [64, P])
        h2_dram = dram("h2_dram", [S, D])
        table_dram = dram("table_dram", [SLOTS * TABLE, 2], I32)
        y_dram = dram("y_dram", [2 * S, D])

        x_rows = A["x"].rearrange("a (t p) d -> (a t) p d", p=P)
        out_rows = out.rearrange("a (t p) d -> (a t) p d", p=P)
        w_ada = A["w_ada"].rearrange("l (p k) n -> p (l k) n", k=KT)
        w_in = A["w_in"].rearrange("l (k p) n -> p (l k) n", p=P)
        w_out = A["w_out"].rearrange("l (k p) n -> p (l k) n", p=P)
        w1 = A["w1"].rearrange("l e (p k) n -> (l e) p (k n)", k=KT)
        w3 = A["w3"].rearrange("l e (p k) n -> (l e) p (k n)", k=KT)
        w2 = A["w2"].rearrange("l e (k p) n -> (l e) p k n", p=P)
        mod_flat = mod_dram.rearrange("a b -> (a b)")

        consts_in = sem("consts_in")
        held = sem("held")
        consts_set = sem("consts_set")
        attn_consts_in = sem("attn_consts_in")
        x_in = [sem(f"x_in{i}") for i in range(2)]
        ada0_in = [sem(f"ada0_in{i}") for i in range(ADA0_RING)]
        c_in = sem("c_in")
        ada0_used = sem("ada0_used")
        ada0_sum = sem("ada0_sum")
        c_exp = sem("c_exp")
        vec_done = sem("vec_done")
        vec_out = sem("vec_out")
        x_square = sem("x_square")
        x_rstd = sem("x_rstd")
        x_normed = sem("x_normed")
        xt_done = sem("xt_done")
        xt_out = sem("xt_out")
        dve_chain = sem("dve_chain")
        act_chain = sem("act_chain")
        pool_chain = sem("pool_chain")
        h_scaled = sem("h_scaled")
        act_rounded = sem("act_rounded")
        act_split = sem("act_split")
        f_in = sem("f_in")
        f_rounded = sem("f_rounded")
        f_split = sem("f_split")
        f_done = sem("f_done")
        f_abs = sem("f_abs")
        f_log = sem("f_log")
        cum_ready = sem("cum_ready")
        w_in_sem = [sem(f"w_in{i}") for i in range(WRING)]
        w_rounded = sem("w_rounded")
        w_split = sem("w_split")
        w_used = sem("w_used")
        ada_in = [sem(f"ada_in{i}") for i in range(2)]
        ada_used = sem("ada_used")
        ada_sum = sem("ada_sum")
        ada_taken = sem("ada_taken")
        z_done = sem("z_done")
        z_out = sem("z_out")
        sq_ready = sem("sq_ready")
        sel_ready = sem("sel_ready")
        rs_ready = sem("rs_ready")
        z_normed = sem("z_normed")
        tr_done = sem("tr_done")
        tr_out = sem("tr_out")
        s_done = sem("s_done")
        s_max = sem("s_max")
        s_exp = sem("s_exp")
        p_normed = sem("p_normed")
        pt_done = sem("pt_done")
        pt_out = sem("pt_out")
        pv_done = sem("pv_done")
        o_out = sem("o_out")
        o_stored = sem("o_stored")
        stage_free = sem("stage_free")
        st_done = sem("st_done")
        st_out = sem("st_out")
        decay_in = [sem(f"decay_in{i}") for i in range(2)]
        decay_used = sem("decay_used")
        rv_done = sem("rv_done")
        rv_out = sem("rv_out")
        gate_out = sem("gate_out")
        gate_log = sem("gate_log")
        gate_exp = sem("gate_exp")
        o_gated = sem("o_gated")
        ot_done = sem("ot_done")
        ot_out = sem("ot_out")
        mod_ready = sem("mod_ready")
        modT_done = sem("modT_done")
        modT_out = sem("modT_out")
        mod_stored = sem("mod_stored")
        o_in = [sem(f"o_in{i}") for i in range(3)]
        x_again = sem("x_again")
        g1_in = [sem(f"g1_in{i}") for i in range(2)]
        mix_out = sem("mix_out")
        x1_ready = sem("x1_ready")
        x1_square = sem("x1_square")
        r2_ready = sem("r2_ready")
        row2_in = sem("row2_in")
        route_in = sem("route_in")
        h2_ready = sem("h2_ready")
        h2_stored = [sem(f"h2_stored{i}") for i in range(2)]
        ms2_ready = sem("ms2_ready")
        h2T_done = sem("h2T_done")
        h2T_out = sem("h2T_out")
        logit_done = sem("logit_done")
        logit_out = sem("logit_out")
        coarse_exp = sem("coarse_exp")
        exp_in = sem("exp_in")
        member_ready = sem("member_ready")
        rank_done = sem("rank_done")
        entries_ready = sem("entries_ready")
        items_ready = sem("items_ready")
        which_in = sem("which_in")
        table_clear = sem("table_clear")
        table_filled = sem("table_filled")
        table_in = sem("table_in")
        m_in = [sem(f"m_in{i}") for i in range(RAW)]
        m_rounded = sem("m_rounded")
        m_split = sem("m_split")
        m_used = sem("m_used")
        idx_ready = sem("idx_ready")
        xg_in = sem("xg_in")
        xgT_done = sem("xgT_done")
        xT_rounded = sem("xT_rounded")
        xT_split = sem("xT_split")
        uv_out = sem("uv_out")
        uvT_done = sem("uvT_done")
        sig_exp = sem("sig_exp")
        a_ready = sem("a_ready")
        a_rounded = sem("a_rounded")
        a_split = sem("a_split")
        y_low_out = sem("y_low_out")
        y_ready = sem("y_ready")
        y_scattered = sem("y_scattered")
        y_free = sem("y_free")
        y_back = [sem(f"y_back{i}") for i in range(2)]
        g2_in = sem("g2_in")
        y0_scaled = sem("y0_scaled")
        fin_ready = sem("fin_ready")
        fin_stored = [sem(f"fin_stored{i}") for i in range(2)]

        block = ctx.enter_context(nc.Block())

        HEAD_CONSTS = 8
        ATTN_CONSTS = 3
        ROUTE_CONSTS = 11

        def extra_pieces(c):
            return 2 if c % 3 == 2 else 1

        def hold(eng, semaphore, value):
            eng.wait_ge(semaphore, value)
            eng.sem_inc(held, 1)

        def wait_z(eng, z, t):
            if t < TT - 1:
                eng.wait_ge(z_done, (TT - 1) * z + t + 1)
            else:
                eng.wait_ge(w_used, WRING + WC * (z + 1))

        def head_out(k):
            if k < 10:
                return o_back[:, k, :]
            return o_back2[:, k - 10, :] if k < 12 else ret_out[:, k - 12, :]

        @block.sync
        def _(sp):
            with sp.Fori(0, ADA0_GROUPS) as g:
                for n in range(KT // 2):
                    hold(sp, ada0_used, KT * g + 2 * n + 2)
                    sp.dma_start(ada0_raw[:, n % ADA0_RING, :].rearrange("p (k n) -> p k n", k=2),
                                 w_ada[:, 2 * n:2 * n + 2, bass.ds(ADA * g, ADA)]).then_inc(ada0_in[n % ADA0_RING], 16)

            def load_w(src, col, c, w0):
                hold(sp, w_split, w0 + c + 1)
                k = 2 * (c % WC)
                sp.dma_start(w_raw[:, c % WRING, :].rearrange("p (k n) -> p k n", k=2),
                             src[:, k:k + 2, bass.ds(col, COLS)]).then_inc(w_in_sem[c % WRING], 16)

            def load_ada(j, a0, group0):
                hold(sp, ada_used, a0 + j + 1)
                sp.dma_start(ada_raw[:, j % 2, :],
                             w_ada[:, j % KT, bass.ds(2 * D + ADA * (group0 + j // KT), ADA)]).then_inc(ada_in[j % 2], 16)

            with sp.Fori(0, GROUPS) as g:
                j = 0
                for c in range(FOX_W):
                    load_w(w_in, FOX_COL[c // WC] + COLS * g, c, FOX_W * g)
                    for _ in range(extra_pieces(c)):
                        load_ada(j, ADA_BODY * g, ADA_GROUPS * g)
                        j += 1
            with sp.Fori(0, GROUPS) as g:
                for c in range(RET_W):
                    load_w(w_in, RET_COL[c // WC] + COLS * g, c, GROUPS * FOX_W + RET_W * g)
                    load_ada(c, ADA_BODY * (GROUPS + g), ADA_GROUPS * (GROUPS + g))
            sp.wait_ge(rv_done, HG * GROUPS)
            sp.wait_ge(o_stored, 16 * (NH + 1))
            for n in range(2):
                sp.dma_start(o_back[:, 5 * n:5 * n + 5, :], o_dram[5 * n:5 * n + 5].rearrange("k p s -> p k s")).then_inc(o_in[n], 16)
            sp.dma_start(o_back2[:, :, :], o_dram[10:12].rearrange("k p s -> p k s")).then_inc(o_in[2], 16)
            w_first = GROUPS * (FOX_W + RET_W)
            with sp.Fori(0, N_OUT) as n:
                for c in range(WC):
                    load_w(w_out, COLS * n, c, w_first + WC * n)

            def load_item(i, e):
                for c in range(ITEM_PIECES):
                    hold(sp, m_split, ITEM_PIECES * i + c + 1)
                    if c < 8:
                        src = (w1, w3)[c % 2][e, :, 4 * DE * (c // 2):4 * DE * (c // 2 + 1)]
                    else:
                        src = w2[e, :, c - 8, :]
                    sp.dma_start(m_raw[:, c % RAW, :], src).then_inc(m_in[c % RAW], 16)

            sp.wait_ge(act_split, 2 * KT)
            with sp.Fori(0, NE) as i:
                load_item(i, i)
            sp.wait_ge(items_ready, 2)
            items = sp.value_load(n_items[0:1, 0:1], min_val=NE, max_val=MAX_ITEMS)
            with sp.If(items > NE):
                with sp.Fori(NE, items) as i:
                    e = sp.value_load(extra_e[0:1, bass.ds(i - NE, 1)], min_val=0, max_val=NE - 1)
                    load_item(i, e)
            with sp.Else():
                sp.nop()
            sp.nop()

        @block.gpsimd
        def _(pool):
            chain = Chain(pool, pool_chain, 0)
            pool.memset(ones[:, :], 1.0).then_inc(consts_set, 1)
            pool.memset(minus_half[:, :], -0.5).then_inc(consts_set, 1)
            pool.memset(f_ones[:, :], 1.0).then_inc(consts_set, 1)
            pool.dma_start(c_cols[:, :], A["c"].rearrange("a (p k) -> (a p) k", k=KT)).then_inc(c_in, 16)
            for t in range(2):
                pool.dma_start(x_st[:, t, :], x_rows[t]).then_inc(x_in[t], 16)
            pool.dma_start(ident[:, :], A["ident"]).then_inc(consts_in, 16)
            pool.dma_start(rot_tab[:, :, :, :], A["rot"]).then_inc(consts_in, 16)
            pool.dma_start(vec_rows[0:96, :], A["b_ada"].rearrange("l (r p) -> (l r) p", p=P)).then_inc(consts_in, 16)
            pool.dma_start(vec_rows[96:112, :], A["norm1_w"].rearrange("l (r p) -> (l r) p", p=P)).then_inc(consts_in, 16)
            pool.dma_start(vec_rows[112:128, :], A["norm2_w"].rearrange("l (r p) -> (l r) p", p=P)).then_inc(consts_in, 16)
            pool.dma_start(head_rows[0:1, :], A["q_norm_w"]).then_inc(consts_in, 16)
            pool.dma_start(head_rows[1:2, :], A["k_norm_w"]).then_inc(consts_in, 16)
            pool.dma_start(head_rows[2:10, :], A["ret_norm_w"].rearrange("l (r p) -> (l r) p", p=P)).then_inc(consts_in, 16)
            with nc.allow_non_contiguous_dma("eight columns"):
                pool.dma_start(f_raw[:, :, :], w_in[:, :, FORGET_COL:FORGET_COL + NH]).then_inc(f_in, 16)
            pool.dma_start(causal[:, :], A["causal"]).then_inc(attn_consts_in, 16)
            pool.dma_start(f_bias[:, :], A["forget_bias"].rearrange("l h -> h l")).then_inc(attn_consts_in, 16)

            def inverse_root(src, dst, n, count):
                chain(pool.tensor_scalar(dst, src, 1.0 / count, EPS, ALU.mult, ALU.add))
                return pool.tensor_tensor(dst, dst, minus_half[:, 0:n], ALU.pow)

            pool.wait_ge(consts_set, 3)
            for t in range(TT):
                pool.wait_ge(x_square, t + 1)
                inverse_root(ssq[:, t:t + 1], rstd[:, t:t + 1], 1, D).then_inc(x_rstd, 1)
                if t + 2 < TT:
                    pool.wait_ge(xt_done, 4 * (t + 1))
                    pool.dma_start(x_st[:, t % 2, :], x_rows[t + 2]).then_inc(x_in[t % 2], 16)
            pool.wait_ge(xt_done, 4 * TT)
            pool.dma_start(one_head[:, :], A["one_head"]).then_inc(attn_consts_in, 16)

            pool.sem_inc(stage_free, 2)
            links = chain.n
            with pool.Fori(0, GROUPS) as g:
                body = Chain(pool, pool_chain, links + 2 * g)
                for n in range(2):
                    hold(pool, sq_ready, 2 * g + n + 1)
                    body(pool.tensor_scalar(rstd[:, :], ssq[:, :], 1.0 / HD, EPS, ALU.mult, ALU.add))
                    pool.tensor_tensor(rstd[:, :], rstd[:, :], minus_half[:, :], ALU.pow).then_inc(rs_ready, 1)
                for h in range(HG):
                    hold(pool, o_out, 1 + HG * g + h + 1)
                    pool.dma_start(o_dram[HG * g + h], o_stage[:, h % 2, :]).then_inc(o_stored, 16)
                    hold(pool, o_stored, 16 * (HG * g + h + 1))
                    pool.sem_inc(stage_free, 1)
            links = links + 2 * GROUPS
            pool.wait_ge(o_out, 1 + HG * GROUPS)
            with pool.Fori(0, GROUPS) as g:
                for h in range(HG):
                    hold(pool, decay_used, HG * g + h + 1)
                    pool.dma_start(decay[:, h % 2, :], A["decay"][HG * g + h]).then_inc(decay_in[h % 2], 16)
                body = Chain(pool, pool_chain, links + HG * g)
                for h in range(HG):
                    hold(pool, sq_ready, 2 * GROUPS + HG * g + h + 1)
                    cols = slice(TT * h, TT * (h + 1))
                    body(pool.tensor_scalar(rstd[:, cols], ssq[:, cols], 1.0 / HD, EPS, ALU.mult, ALU.add))
                    pool.tensor_tensor(rstd[:, cols], rstd[:, cols], minus_half[:, 0:TT], ALU.pow).then_inc(rs_ready, 1)
                hold(pool, ot_out, HG * g + HG)
                pool.dma_start(o_dram[bass.ds(NH + HG * g, HG)].rearrange("k p s -> p k s"), ret_out[:, :, :]).then_inc(o_stored, 16)
            links = links + HG * GROUPS
            chain = Chain(pool, pool_chain, links)
            pool.wait_ge(modT_out, 1)
            pool.dma_start(mod_dram, mod_rows_sb[:, :]).then_inc(mod_stored, 16)
            pool.wait_ge(mod_stored, 16)
            pool.wait_ge(act_split, 2 * KT)
            pool.wait_ge(o_stored, 16 * (NH + GROUPS))
            for t in range(TT):
                pool.dma_start(x1[:, t, :], x_rows[t]).then_inc(x_again, 16)
            pool.dma_start(shift2[:, :], mod_flat[D:2 * D].partition_broadcast(P)).then_inc(row2_in, 16)
            pool.dma_start(scale2[:, :], mod_flat[2 * D:3 * D].partition_broadcast(P)).then_inc(row2_in, 16)
            with pool.Fori(0, N_OUT // 2) as m:
                for s in range(2):
                    hold(pool, mix_out, TT * (2 * m + s) + 1)
                    pool.dma_start(g1_row[:, s, :],
                                   mod_flat[bass.ds(COLS * (2 * m + s), COLS)].partition_broadcast(P)).then_inc(g1_in[s], 16)
            pool.wait_ge(ms2_ready, 1)
            chain(pool.tensor_scalar(ms2[:, :], ms2[:, :], 1.0 / D, EPS, ALU.mult, ALU.add))
            pool.tensor_tensor(r2[:, :], ms2[:, :], minus_half[:, 0:TT], ALU.pow).then_inc(r2_ready, 1)
            pool.memset(ones2[:, :], 1.0).then_inc(consts_set, 1)
            pool.dma_start(table_dram, A["table0"].rearrange("s (i c) -> (s i) c", c=2)).then_inc(table_clear, 16)
            pool.dma_start(route_w[:, :, 0:NG], A["w_coarse"].rearrange("l (p k) g -> (l p) k g", k=KT)).then_inc(route_in, 16)
            for gr in range(NG):
                pool.dma_start(route_w[:, :, NG + EPG * gr:NG + EPG * (gr + 1)],
                               A["w_fine"][0, gr].rearrange("(p k) e -> p k e", k=KT)).then_inc(route_in, 16)
            pool.dma_start(route_b[:, 0:NG], A["b_coarse"].to_broadcast([P, NG])).then_inc(route_in, 16)
            pool.dma_start(route_b[:, NG:], A["b_fine"].rearrange("l g e -> l (g e)").to_broadcast([P, NE])).then_inc(route_in, 16)
            pool.dma_start(strict[:, :], A["strict"]).then_inc(route_in, 16)
            pool.dma_start(iota[:, :], A["iota"]).then_inc(route_in, 16)
            pool.dma_start(twice[:, :], A["twice"]).then_inc(route_in, 16)
            pool.dma_start(pair[:, :], A["pair"]).then_inc(route_in, 16)
            for t in range(TT):
                pool.wait_ge(h2_ready, t + 1)
                pool.dma_start(h2_dram[P * t:P * (t + 1), :], h2[:, t % 2, :]).then_inc(h2_stored[t % 2], 16)
                if t == 0:
                    pool.memset(xg[:, :], 0.0).then_inc(consts_set, 1)
            pool.wait_ge(h2_stored[0], 8 * TT)
            pool.wait_ge(h2_stored[1], 8 * TT)
            pool.wait_ge(h2T_done, 4 * TT)
            pool.dma_start(which[:, :], A["which"]).then_inc(which_in, 16)
            pool.wait_ge(table_clear, 16)
            pool.wait_ge(entries_ready, 1)
            for n in range(2 * TT):
                pool.indirect_dma_start(out=table_dram, out_offset=bass.IndirectOffsetOnAxis(ap=slot_i[:, n:n + 1], axis=0),
                                        in_=entry[:, n, :], in_offset=None,
                                        bounds_check=SLOTS * TABLE - 1, oob_is_err=False).then_inc(table_filled, 16)
            pool.wait_ge(table_filled, 32 * TT)
            pool.dma_start(table[:, :, :], table_dram.rearrange("(s i) c -> s i c", i=TABLE)).then_inc(table_in, 16)
            pool.wait_ge(table_in, 16)
            pool.wait_ge(items_ready, 2)
            items = pool.value_load(n_items[0:1, 0:1], min_val=NE, max_val=MAX_ITEMS)
            pool.wait_ge(consts_set, 5)

            def gather():
                pool.indirect_dma_start(out=xg[:, :], out_offset=None, in_=h2_dram,
                                        in_offset=bass.IndirectOffsetOnAxis(ap=idx_in[:, 0:1], axis=0),
                                        bounds_check=S - 1, oob_is_err=False).then_inc(xg_in, 16)

            pool.tensor_copy(idx_in[:, :], table[:, 1, 0:1]).then_inc(idx_ready, 1)
            pool.wait_ge(idx_ready, 1)
            gather()
            pool.sem_inc(y_free, 1)

            def scatter(column, n):
                pool.tensor_copy(idx_out[:, :], table[:, bass.ds(column, 1), 1:2]).then_inc(idx_ready, 1)
                hold(pool, idx_ready, n)
                hold(pool, y_ready, column + 2)
                pool.indirect_dma_start(out=y_dram, out_offset=bass.IndirectOffsetOnAxis(ap=idx_out[:, 0:1], axis=0),
                                        in_=y_sb[:, :], in_offset=None,
                                        bounds_check=2 * S - 1, oob_is_err=False).then_inc(y_scattered, 16)
                hold(pool, y_scattered, 16 * column + 16)

            with pool.Fori(0, items) as i:
                hold(pool, xgT_done, 2 * i + 2)
                hold(pool, xg_in, 16 * i + 16)
                pool.tensor_copy(idx_in[:, :], table[:, bass.ds(i + 2, 1), 0:1]).then_inc(idx_ready, 1)
                hold(pool, idx_ready, 2 * i + 2)
                gather()
                scatter(i, 2 * i + 3)
                pool.sem_inc(y_free, 1)
            scatter(items, 2 * items + 2)
            hold(pool, xg_in, 16 * items + 16)
            y_rows = y_dram.rearrange("(t p k) d -> t p k d", p=P, k=2)
            hold(pool, m_used, SPL + ITEM_PIECES * items)
            hold(pool, xgT_done, 2 * items + 2)
            pool.dma_start(g2_row[:, :], mod_flat[3 * D:4 * D].partition_broadcast(P)).then_inc(g2_in, 16)
            for t in range(2):
                pool.dma_start(y_in[:, t, :, :], y_rows[t]).then_inc(y_back[t], 16)
            for t in range(TT):
                pool.wait_ge(fin_ready, t + 1)
                pool.dma_start(out_rows[t], fin[:, t % 2, :]).then_inc(fin_stored[t % 2], 16)
                if t + 2 < TT:
                    pool.dma_start(y_in[:, t % 2, :, :], y_rows[t + 2]).then_inc(y_back[t % 2], 16)
            pool.wait_ge(fin_stored[0], 16 * TT // 2)
            pool.wait_ge(fin_stored[1], 16 * TT // 2)

        @block.scalar
        def _(act):
            chain = Chain(act, act_chain, 0)
            act.sem_inc(xt_out, 4)
            act.wait_ge(c_in, 16)
            act.activation(c_tmp[:, :], c_cols[:, :], ACT.Exp, scale=-1.0).then_inc(c_exp, 1)
            for t in range(TT):
                act.wait_ge(x_in[t % 2], 16 * (t // 2 + 1))
                if t > 0:
                    act.wait_ge(x_square, t)
                act.activation(square_out[:, :], x_st[:, t % 2, :], ACT.Square, accum_out=ssq[:, t:t + 1]).then_inc(x_square, 1)
                if t > 0:
                    for q in range(4):
                        act.wait_ge(xt_done, 4 * (t - 1) + q + 1)
                        act.activation(act32[:, 4 * q:4 * q + 4, P * (t - 1):P * t],
                                       psum[:, q, :].rearrange("p (k s) -> p k s", k=4), ACT.Copy).then_inc(xt_out, 1)
            for q in range(4):
                act.wait_ge(xt_done, 4 * (TT - 1) + q + 1)
                act.activation(act32[:, 4 * q:4 * q + 4, P * (TT - 1):P * TT],
                               psum[:, q, :].rearrange("p (k s) -> p k s", k=4), ACT.Copy).then_inc(xt_out, 1)
            act.wait_ge(f_in, 16)
            act.activation(f_hi[:, :, :], f_raw[:, :, :], ACT.Copy).then_inc(f_rounded, 1)
            for k in range(KT):
                act.wait_ge(h_scaled, k + 1)
                act.activation(act_hi[:, k, :], act32[:, k, :], ACT.Copy).then_inc(act_rounded, 1)
            act.wait_ge(f_abs, 1)
            chain(act.activation(f_e[:, :], f_e[:, :], ACT.Exp))
            act.activation(f_e[:, :], f_e[:, :], ACT.Ln, bias=ones[0:NH, :]).then_inc(f_log, 1)

            def round_w(c, w0, r0):
                act.wait_ge(w_in_sem[c % WRING], 16 * (r0 + c // WRING + 1))
                act.wait_ge(w_used, w0 + c + 1)
                act.activation(w_hi[:, c % WRING, :], w_raw[:, c % WRING, :], ACT.Copy).then_inc(w_rounded, 1)

            def take_z(dst, z):
                for t in range(TT):
                    wait_z(act, z, t)
                    act.activation(dst[:, t, :], psum[:, t, :], ACT.Copy).then_inc(z_out, 1)

            def take_heads(dst, n, h, scale):
                act.wait_ge(tr_done, n + 1)
                act.activation(dst[:, h, :], psum[:, 6 + h % 2, :], ACT.Copy, scale=scale).then_inc(tr_out, 1)

            def attention_act(p, g):
                if p < UNITS // 2:
                    for u in (2 * p, 2 * p + 1):
                        n = P * (u % TT + 1)
                        act.wait_ge(s_max, UNITS * g + u + 1)
                        act.wait_ge(pt_done, UNITS * g + u + 1)
                        act.activation(probs[:, u % 2, 0:n], psum[:, 4 + u % 2, 0:n], ACT.Exp,
                                       bias=row_max[:, u % 2:u % 2 + 1], accum_out=row_sum[:, u % 2:u % 2 + 1]).then_inc(s_exp, 1)
                if p > 0:
                    for u in (2 * p - 2, 2 * p - 1):
                        n = P * (u % TT + 1)
                        start = (0, 1, 3, 6)[u % TT] * P
                        act.wait_ge(pt_done, 2 + UNITS * g + u + 1)
                        act.activation(pT[:, u // TT, start:start + n], psum[:, 6 + u % 2, 0:n], ACT.Copy).then_inc(pt_out, 1)

            act.sem_inc(z_out, TT)
            act.sem_inc(tr_out, 2)
            act.sem_inc(s_exp, 2)
            act.sem_inc(pt_out, 2)
            act.sem_inc(o_out, 1)
            act.sem_inc(rv_out, 2)
            with act.Fori(0, GROUPS) as g:
                z0 = FOX_CHUNKS * g
                for c in range(FOX_W):
                    round_w(c, FOX_W * g, FOX_W // WRING * g)
                    if c == 9:
                        take_z(zst, z0)
                    if 13 <= c <= 16:
                        take_heads(kT, 8 * g + c - 13, c - 13, head_cols[:, 1:2])
                    if c == 17:
                        take_z(zst, z0 + 1)
                    if c in (19, 20):
                        for h in (2 * (c - 19), 2 * (c - 19) + 1):
                            take_heads(qT, 8 * g + HG + h, h, head_cols[:, 0:1])
                    if c >= 21:
                        attention_act(2 * (c - 21), g)
                        attention_act(2 * (c - 21) + 1, g)
                attention_act(6, g)
                attention_act(7, g)
                take_z(v_sb, z0 + 2)
                attention_act(8, g)
                for h in range(HG):
                    act.wait_ge(pv_done, HG * g + h + 1)
                    act.wait_ge(stage_free, HG * g + h + 1)
                    act.activation(o_stage[:, h % 2, :], psum[:, 4 + h, :], ACT.Copy).then_inc(o_out, 1)
            with act.Fori(0, GROUPS) as g:
                z0 = Z_RET + RET_CHUNKS * g
                for c in range(RET_W):
                    round_w(c, GROUPS * FOX_W + RET_W * g, GROUPS * FOX_W // WRING + RET_W // WRING * g)
                    if c == 9:
                        take_z(zst, z0)
                    if 13 <= c <= 16:
                        take_heads(qT, 16 + 8 * g + c - 13, c - 13, 1.0)
                    if c == 17:
                        take_z(zst, z0 + 1)
                    if c in (19, 20):
                        act.wait_ge(o_stored, 16 * (NH + g))
                        for h in (2 * (c - 19), 2 * (c - 19) + 1):
                            take_heads(kT, 16 + 8 * g + HG + h, h, 1.0)
                    if c == 25:
                        take_z(v_sb, z0 + 2)
                    if 27 <= c <= 30:
                        h = c - 27
                        act.wait_ge(rv_done, HG * g + h + 1)
                        act.activation(o_sb[:, h, :, :], psum[:, 6 + h % 2, :].rearrange("p (t d) -> p t d", d=HD), ACT.Copy).then_inc(rv_out, 1)
                for t in range(TT):
                    wait_z(act, z0 + 3, t)
                    act.activation(gate[:, t, :], psum[:, t, :], ACT.Copy).then_inc(gate_out, 1)
                    act.activation(zst[:, t, :], psum[:, t, :], ACT.Exp, scale=-1.0).then_inc(z_out, 1)
                for n in range(2):
                    tiles = slice(2 * n, 2 * n + 2)
                    act.wait_ge(z_out, TT * (z0 + 3) + TT + 2 * n + 2)
                    act.activation(zst[:, tiles, :], zst[:, tiles, :], ACT.Ln, bias=ones[:, :]).then_inc(gate_log, 1)
                for n in range(2):
                    tiles = slice(2 * n, 2 * n + 2)
                    act.wait_ge(gate_log, 2 * g + n + 1)
                    act.activation(zst[:, tiles, :], zst[:, tiles, :], ACT.Exp, scale=-1.0).then_inc(gate_exp, 1)
                for h in range(HG):
                    act.wait_ge(ot_done, HG * g + h + 1)
                    act.activation(ret_out[:, h, :], psum[:, 4 + h, :], ACT.Copy,
                                   scale=head_cols[:, bass.ds(2 + HG * g + h, 1)]).then_inc(ot_out, 1)
            act.wait_ge(modT_done, 1)
            act.activation(mod_rows_sb[:, :], psum[0:64, 5, 0:P], ACT.Copy).then_inc(modT_out, 1)
            for k in range(KT):
                if k in (0, 5, 10):
                    act.wait_ge(o_in[k // 5], 16)
                if k == 12:
                    act.wait_ge(ot_out, HG * GROUPS)
                act.activation(act_hi[:, k, :], head_out(k), ACT.Copy).then_inc(act_rounded, 1)
            w_first = GROUPS * (FOX_W + RET_W)

            def square_x1(n):
                for t in range(TT):
                    act.wait_ge(x1_ready, TT * n + t + 1)
                    act.wait_ge(x1_square, TT * n + t + 1)
                    act.activation(sq2[:, :], x1[:, t, bass.ds(COLS * n, COLS)], ACT.Square,
                                   accum_out=ss2[:, t, bass.ds(n, 1)]).then_inc(x1_square, 1)

            act.sem_inc(x1_square, 1)
            with act.Fori(0, N_OUT // 2) as m:
                for c in range(2 * WC):
                    round_w(c, w_first + 2 * WC * m, w_first // WRING + 2 * WC // WRING * m)
                    if c == WC + 1:
                        square_x1(2 * m)
                square_x1(2 * m + 1)
            for t in range(TT):
                for q in range(4):
                    act.wait_ge(h2T_done, 4 * t + q + 1)
                    if q == 0 and t > 0:
                        act.wait_ge(logit_done, t)
                    act.activation(h2T[:, 4 * q:4 * q + 4, :], psum[:, q, :].rearrange("p (k s) -> p k s", k=4), ACT.Copy).then_inc(h2T_out, 1)
            act.wait_ge(exp_in, 1)
            act.activation(r_exp[:, :], r_exp[:, :], ACT.Exp).then_inc(coarse_exp, 1)

            def round_x(half, n):
                act.wait_ge(xgT_done, n + 1)
                act.activation(xT[:, 8 * half:8 * half + 8, 0, :], psum[:, 6, :].rearrange("p (k s) -> p k s", s=SLOTS), ACT.Copy).then_inc(xT_rounded, 1)

            act.wait_ge(items_ready, 2)
            items = act.value_load(n_items[0:1, 0:1], min_val=NE, max_val=MAX_ITEMS)
            act.sem_inc(uv_out, 1)
            act.wait_ge(logit_done, TT)
            round_x(0, 0)
            round_x(1, 1)

            def take_y_low(i):
                act.wait_ge(m_used, SPL + ITEM_PIECES * i)
                act.wait_ge(y_ready, i + 1)
                act.activation(y_low[:, :].rearrange("p (b n) -> p b n", b=4), psum[SLOTS:P, 0:4, :], ACT.Copy).then_inc(y_low_out, 1)

            with act.Fori(0, items) as i:
                for c in range(ITEM_PIECES):
                    act.wait_ge(m_in[c % RAW], 32 * i + 16 * (c // RAW + 1))
                    act.wait_ge(m_used, ITEM_PIECES * i + c + 1)
                    act.activation(m_hi[:, c % SPL, :], m_raw[:, c % RAW, :], ACT.Copy).then_inc(m_rounded, 1)
                    if c == Y_AFTER:
                        take_y_low(i)
                    if c == UV_AFTER:
                        act.wait_ge(m_used, SPL + ITEM_PIECES * i + 8)
                        act.activation(uv_sb[:, :, :], psum[:, 4:6, :], ACT.Copy).then_inc(uv_out, 1)
                        round_x(0, 2 * i + 2)
                    if c == SILU_AFTER:
                        act.wait_ge(uvT_done, i + 1)
                        act.activation(sig[:, :, :], psum[:, 7, 0:FT * SLOTS].rearrange("p (f s) -> p f s", s=SLOTS), ACT.Exp, scale=-1.0).then_inc(sig_exp, 1)
                        round_x(1, 2 * i + 3)
                    if c == A_AFTER:
                        act.wait_ge(a_ready, i + 1)
                        act.activation(aT[:, :, 0, :], aT32[:, :, :], ACT.Copy).then_inc(a_rounded, 1)
            take_y_low(items)
            for t in range(TT):
                act.wait_ge(y_back[t % 2], 16 * (t // 2 + 1))
                if t >= 2:
                    act.wait_ge(fin_stored[t % 2], 16 * (t // 2))
                act.activation(fin[:, t % 2, :], y_in[:, t % 2, 0, :], ACT.Copy, scale=gates[:, t, 0:1]).then_inc(y0_scaled, 1)

        @block.vector
        def _(dve):
            chain = Chain(dve, dve_chain, 0)
            dve.sem_inc(ada0_used, 2 * ADA0_RING)
            dve.sem_inc(w_split, WRING)
            dve.sem_inc(ada_used, 2)
            chain(dve.memset(ada_acc[:, :], 0.0))
            dve.wait_ge(c_exp, 1)
            chain(dve.tensor_scalar(c_tmp[:, :], c_tmp[:, :], 1.0, None, ALU.add))
            chain(dve.reciprocal(c_tmp[:, :], c_tmp[:, :]))
            chain(dve.tensor_tensor(c_cols[:, :], c_cols[:, :], c_tmp[:, :], ALU.mult))
            dve.wait_ge(vec_done, 1)
            chain(dve.tensor_copy(vec_cols[:, :], psum[:, 0, 0:P]))
            chain(dve.tensor_copy(head_cols[:, :], psum[:, 1, 0:10]))
            dve.tensor_scalar(head_cols[:, 0:1], head_cols[:, 0:1], HD ** -0.5, None, ALU.mult).then_inc(vec_out, 1)
            with dve.Fori(0, ADA0_GROUPS // 2) as m:
                for a in range(2):
                    for k in range(KT):
                        n = k // 2
                        src = ada0_raw[:, n % ADA0_RING, ADA * (k % 2):ADA * (k % 2 + 1)]
                        if k % 2 == 0:
                            dve.wait_ge(ada0_in[n % ADA0_RING], 64 * m + 32 * a + 16 * (n // ADA0_RING + 1))
                        if k == 0:
                            dve.wait_ge(ada0_sum, 2 * m + a + 1)
                            dve.tensor_scalar(ada0_acc[:, a, :], src, c_cols[:, 0:1], None, ALU.mult).then_inc(ada0_used, 1)
                        else:
                            dve.wait_ge(ada0_used, 2 * ADA0_RING + 2 * KT * m + KT * a + k)
                            dve.scalar_tensor_tensor(ada0_acc[:, a, :], src, c_cols[:, k:k + 1], ada0_acc[:, a, :],
                                                     ALU.mult, ALU.add).then_inc(ada0_used, 1)
                        if k == 3:
                            dve.wait_ge(x_rstd, 2 * m + a + 1)
                            dve.tensor_scalar(x_st[:, a, :], x_st[:, a, :], rstd[:, bass.ds(2 * m + a, 1)], None, ALU.mult).then_inc(x_normed, 1)

            def scale_h(k):
                dve.tensor_scalar(act32[:, k, :], act32[:, k, :], mod_cols[:, 16 + k:17 + k], mod_cols[:, k:k + 1],
                                  ALU.mult, ALU.add).then_inc(h_scaled, 1)

            dve.wait_ge(f_rounded, 1)
            dve.tensor_tensor(f_lo[:, :, :], f_raw[:, :, :], f_hi[:, :, :].bitcast(F32), ALU.subtract).then_inc(f_split, 1)
            dve.wait_ge(xt_out, 4 + 4 * TT)
            dve.wait_ge(ada0_sum, 2 + 3)
            chain(dve.tensor_tensor(mod_cols[:, 0:24].rearrange("p (g j) -> p g j", j=8), psum[:, 4:7, 0:8],
                                    vec_cols[:, 0:24].rearrange("p (g j) -> p g j", j=8), ALU.add))
            chain(dve.scalar_tensor_tensor(mod_cols[:, 16:24], mod_cols[:, 16:24], 1.0, vec_cols[:, 96:104], ALU.add, ALU.mult))
            for k in range(KT // 2):
                scale_h(k)
            dve.wait_ge(ada0_sum, 2 + 4)
            chain(dve.tensor_tensor(mod_cols[:, 24:32], psum[:, 7, 0:8], vec_cols[:, 24:32], ALU.add))
            chain(dve.scalar_tensor_tensor(mod_cols[:, 24:32], mod_cols[:, 24:32], 1.0, vec_cols[:, 104:112], ALU.add, ALU.mult))
            for k in range(KT):
                if k < KT // 2:
                    scale_h(KT // 2 + k)
                dve.wait_ge(act_rounded, k + 1)
                dve.tensor_tensor(act_lo[:, k, :], act32[:, k, :], act_hi[:, k, :].bitcast(F32), ALU.subtract).then_inc(act_split, 1)
            dve.wait_ge(attn_consts_in, 16 * ATTN_CONSTS)
            dve.wait_ge(f_done, 1)
            chain(dve.tensor_scalar(f_y[:, :], psum[0:NH, 4, :], f_bias[:, 0:1], None, ALU.add))
            chain(dve.tensor_scalar(f_e[:, :], f_y[:, :], -1.0, None, ALU.mult))
            dve.tensor_tensor(f_e[:, :], f_e[:, :], f_y[:, :], ALU.min).then_inc(f_abs, 1)
            dve.wait_ge(f_abs, 1)
            chain(dve.tensor_scalar(f_y[:, :], f_y[:, :], 0.0, None, ALU.min))
            dve.wait_ge(f_log, 1)
            chain(dve.tensor_tensor(f_e[:, :], f_e[:, :], f_y[:, :], ALU.subtract))
            dve.wait_ge(consts_set, 3)
            dve.tensor_tensor_scan(neg_cum[:, :], f_ones[:, :], f_e[:, :], 0.0, ALU.mult, ALU.add).then_inc(cum_ready, 1)

            def split_w(c, w0):
                dve.wait_ge(w_rounded, w0 + c + 1)
                dve.tensor_tensor(w_lo[:, c % WRING, :], w_raw[:, c % WRING, :], w_hi[:, c % WRING, :].bitcast(F32),
                                  ALU.subtract).then_inc(w_split, 1)

            def sum_ada(j, a0, r0):
                dve.wait_ge(ada_in[j % 2], r0 + 16 * (j // 2 + 1))
                dve.wait_ge(ada_used, a0 + j + 2)
                dve.scalar_tensor_tensor(ada_acc[:, :], ada_raw[:, j % 2, :], c_cols[:, j % KT:j % KT + 1], ada_acc[:, :],
                                         ALU.mult, ALU.add).then_inc(ada_used, 1)

            def take_ada(group, bank, chain):
                dve.wait_ge(ada_sum, group + 1)
                at8 = bass.ds(32 + 8 * group, 8)
                dve.tensor_tensor(mod_cols[:, at8], psum[:, bank, 0:8], vec_cols[:, at8], ALU.add).then_inc(ada_taken, 1)
                chain(dve.memset(ada_acc[:, :], 0.0))

            def norm_heads(n, z, chain):
                dve.wait_ge(z_out, TT * z + 2 * TT)
                for t in range(TT):
                    chain(dve.tensor_tensor(sq[:, :], zst[:, t, :], zst[:, t, :], ALU.mult))
                    r = dve.tensor_reduce(ssq[:, HG * t:HG * t + HG], sq[:, :].rearrange("p (h d) -> p h d", d=HD), AX.X, ALU.add)
                    if t < TT - 1:
                        chain(r)
                r.then_inc(sq_ready, 1)
                dve.wait_ge(rs_ready, n + 1)
                zv = zst[:, :, :].rearrange("p t (h d) -> p (t h) d", d=HD)
                dve.tensor_tensor(zv, zv, rstd[:, :].unsqueeze(2).broadcast_to([P, KT, HD]), ALU.mult).then_inc(z_normed, 1)

            def attention_dve(p, g, chain):
                for u in (2 * p, 2 * p + 1):
                    n = P * (u % TT + 1)
                    dve.wait_ge(s_done, UNITS * g + u + 1)
                    dve.tensor_reduce(row_max[:, u % 2:u % 2 + 1], psum[:, 4 + u % 2, 0:n], AX.X, ALU.max, negate=True).then_inc(s_max, 1)
                for u in (2 * p, 2 * p + 1):
                    n = P * (u % TT + 1)
                    dve.wait_ge(s_exp, 2 + UNITS * g + u + 1)
                    chain(dve.reciprocal(row_inv[:, u % 2:u % 2 + 1], row_sum[:, u % 2:u % 2 + 1]))
                    dve.tensor_scalar(probs[:, u % 2, 0:n], probs[:, u % 2, 0:n], row_inv[:, u % 2:u % 2 + 1], None,
                                      ALU.mult).then_inc(p_normed, 1)

            links = chain.n
            per_body = 2 * (2 * TT - 1) + UNITS + ADA_GROUPS
            with dve.Fori(0, GROUPS) as g:
                body = Chain(dve, dve_chain, links + per_body * g)
                z0 = FOX_CHUNKS * g
                dve.tensor_copy(head_sel[:, :], one_head[:, bass.ds(HG * P * g, HG * P)]).then_inc(sel_ready, 1)
                j = 0
                for c in range(FOX_W):
                    split_w(c, FOX_W * g)
                    for _ in range(extra_pieces(c)):
                        if j == KT:
                            take_ada(ADA_GROUPS * g, 5, body)
                        sum_ada(j, ADA_BODY * g, 16 * ADA_BODY // 2 * g)
                        j += 1
                    if c == 9:
                        norm_heads(2 * g, z0, body)
                    if c == 17:
                        norm_heads(2 * g + 1, z0 + 1, body)
                    if c >= 21:
                        attention_dve(2 * (c - 21), g, body)
                        attention_dve(2 * (c - 21) + 1, g, body)
                attention_dve(6, g, body)
                attention_dve(7, g, body)
                take_ada(ADA_GROUPS * g + 1, 0, body)
                assert body.n == per_body, body.n
            links += per_body * GROUPS

            def rotate(z, chain):
                dve.wait_ge(z_out, TT * z + 2 * TT)
                zh = zst[:, :, :].rearrange("p t (h c d) -> p t h c d", h=HG, c=2)
                cos, sin = (rot_tab[:, n, :, :].unsqueeze(2).broadcast_to([P, TT, HG, HD // 2]) for n in range(2))
                z1, z2, r1, r2_ = zh[:, :, :, 0, :], zh[:, :, :, 1, :], rot[:, :, :, 0, :], rot[:, :, :, 1, :]
                dve.tensor_tensor(r1, z1, cos, ALU.mult)
                chain(dve.tensor_tensor(r2_, z1, sin, ALU.mult))
                chain(dve.tensor_tensor(z1, z2, sin, ALU.mult))
                chain(dve.tensor_tensor(z2, z2, cos, ALU.mult))
                chain(dve.tensor_tensor(r1, r1, z1, ALU.subtract))
                dve.tensor_tensor(r2_, r2_, z2, ALU.add).then_inc(z_normed, 1)

            def decay_scores(u, g):
                h, jt = u // TT, u % TT
                n = S - P * jt
                if jt == 0:
                    dve.wait_ge(decay_in[h % 2], 32 * g + 16 * (h // 2) + 16)
                dve.wait_ge(st_done, UNITS * g + u + 1)
                start = (0, 512, 896, 1152)[jt]
                dve.tensor_tensor(pT[:, h, start:start + n], psum[:, 4 + u % 2, 0:n], decay[:, h % 2, 0:n], ALU.mult).then_inc(st_out, 1)
                if jt == TT - 1:
                    dve.wait_ge(st_out, 2 + UNITS * g + u + 1)
                    dve.sem_inc(decay_used, 1)

            def norm_retention(h, g, chain):
                dve.wait_ge(rv_out, 2 + HG * g + h + 1)
                ov = o_sb[:, h, :, :]
                chain(dve.tensor_tensor(sq[:, :], ov.rearrange("p t d -> p (t d)"), ov.rearrange("p t d -> p (t d)"), ALU.mult))
                cols = slice(TT * h, TT * (h + 1))
                dve.tensor_reduce(ssq[:, cols], sq[:, :].rearrange("p (t d) -> p t d", d=HD), AX.X, ALU.add).then_inc(sq_ready, 1)
                dve.wait_ge(rs_ready, 2 * GROUPS + HG * g + h + 1)
                chain(dve.tensor_tensor(ov, ov, rstd[:, cols].unsqueeze(2).broadcast_to([P, TT, HD]), ALU.mult))

            dve.sem_inc(st_out, 2)
            dve.sem_inc(decay_used, 2)
            per_body = 2 * 4 + 2 * HG + ADA_GROUPS + HG
            with dve.Fori(0, GROUPS) as g:
                body = Chain(dve, dve_chain, links + per_body * g)
                z0 = Z_RET + RET_CHUNKS * g
                group0 = ADA_GROUPS * (GROUPS + g)
                for c in range(RET_W):
                    split_w(c, GROUPS * FOX_W + RET_W * g)
                    if c == KT:
                        take_ada(group0, 5, body)
                    sum_ada(c, ADA_BODY * (GROUPS + g), 16 * ADA_BODY // 2 * (GROUPS + g))
                    if c == 9:
                        rotate(z0, body)
                    if c == 17:
                        rotate(z0 + 1, body)
                    if 21 <= c <= 24:
                        for u in range(4 * (c - 21), 4 * (c - 21) + 4):
                            decay_scores(u, g)
                    if 28 <= c <= 31:
                        norm_retention(c - 28, g, body)
                take_ada(group0 + 1, 0, body)
                dve.wait_ge(gate_out, TT * g + TT)
                for h in range(HG):
                    body(dve.tensor_tensor(o_sb[:, h, :, :], o_sb[:, h, :, :], gate[:, :, HD * h:HD * (h + 1)], ALU.mult))
                for n in range(2):
                    tiles = slice(2 * n, 2 * n + 2)
                    dve.wait_ge(gate_exp, 2 * g + n + 1)
                    ov = o_sb[:, :, tiles, :].rearrange("p h t d -> p t h d")
                    dve.tensor_tensor(ov, ov, zst[:, tiles, :].rearrange("p t (h d) -> p t h d", h=HG), ALU.mult).then_inc(o_gated, 1)
                assert body.n == per_body, body.n
            links += per_body * GROUPS
            chain = Chain(dve, dve_chain, links)
            dve.wait_ge(ada_taken, 2 * ADA_GROUPS * GROUPS)
            dve.scalar_tensor_tensor(mod_cols[:, 64:80], mod_cols[:, 64:80], 1.0, vec_cols[:, 112:128], ALU.add, ALU.mult).then_inc(mod_ready, 1)
            for k in range(KT):
                dve.wait_ge(act_rounded, KT + k + 1)
                dve.tensor_tensor(act_lo[:, k, :], head_out(k), act_hi[:, k, :].bitcast(F32), ALU.subtract).then_inc(act_split, 1)
            w_first = GROUPS * (FOX_W + RET_W)

            def add_mix(n, s, m):
                dve.wait_ge(g1_in[s], 16 * m + 16)
                dve.wait_ge(x_again, 16 * TT)
                for t in range(TT):
                    wait_z(dve, Z_OUT + n, t)
                    dve.tensor_tensor(mix_tmp[:, :], psum[:, t, :], g1_row[:, s, :], ALU.mult).then_inc(mix_out, 1)
                    dve.wait_ge(mix_out, TT + TT * n + t + 1)
                    x1c = x1[:, t, bass.ds(COLS * n, COLS)]
                    dve.tensor_tensor(x1c, x1c, mix_tmp[:, :], ALU.add).then_inc(x1_ready, 1)
                    dve.wait_ge(x1_ready, TT * n + t + 1)

            dve.sem_inc(mix_out, TT)
            with dve.Fori(0, N_OUT // 2) as m:
                for c in range(2 * WC):
                    split_w(c, w_first + 2 * WC * m)
                    if c == WC + 1:
                        add_mix(2 * m, 0, m)
                add_mix(2 * m + 1, 1, m)
            dve.sem_inc(m_split, 4)
            dve.wait_ge(x1_square, 1 + TT * N_OUT)
            dve.tensor_reduce(ms2[:, :], ss2[:, :, :], AX.X, ALU.add).then_inc(ms2_ready, 1)
            dve.wait_ge(r2_ready, 1)
            dve.wait_ge(row2_in, 32)
            for t in range(TT):
                if t >= 2:
                    dve.wait_ge(h2_stored[t % 2], 16)
                    dve.wait_ge(h2T_done, 4 * (t - 1))
                h2v = h2[:, t % 2, :].rearrange("p (k q) -> p q k", k=KT)
                nat = "p (q k) -> p q k"
                chain(dve.scalar_tensor_tensor(h2v, x1[:, t, :].rearrange(nat, k=KT), r2[:, t:t + 1], scale2[:, :].rearrange(nat, k=KT),
                                               ALU.mult, ALU.mult))
                dve.tensor_tensor(h2v, h2v, shift2[:, :].rearrange(nat, k=KT), ALU.add).then_inc(h2_ready, 1)
            dve.wait_ge(h2_ready, TT)
            dve.sem_inc(m_split, 2)
            dve.wait_ge(route_in, 16 * ROUTE_CONSTS)
            for t in range(TT):
                dve.wait_ge(logit_done, t + 1)
                chain(dve.tensor_tensor(logit[:, t, :], psum[:, 4 + t, 0:NG + NE], route_b[:, :], ALU.add))
            chain(dve.memset(coarse8[:, :], -BIG))
            for t in range(TT):
                chain(dve.tensor_copy(coarse8[:, 0:NG], logit[:, t, 0:NG]))
                chain(dve.max(top8[:, 0, :], coarse8[:, :]))
                chain(dve.max_index(idx8[:, 0, :], top8[:, 0, :], coarse8[:, :]))
                chain(dve.tensor_scalar(r_exp[:, NG * t:NG * t + NG], logit[:, t, 0:NG], top8[:, 0, 0:1], None, ALU.subtract))
                chain(dve.tensor_copy(small[:, 0:1], idx8[:, 0, 0:1]))
                chain(dve.tensor_scalar(small[:, 4:8], iota[:, 0:NG], small[:, 0:1], -1.0, ALU.is_equal, ALU.add))
                chain(dve.tensor_scalar(small[:, 8:12], small[:, 4:8], BIG, None, ALU.mult))
                chain(dve.tensor_tensor(fine[:, :].rearrange("p (g e) -> p g e", g=NG),
                                        logit[:, t, NG:].rearrange("p (g e) -> p g e", g=NG),
                                        small[:, 8:12].unsqueeze(2).broadcast_to([P, NG, EPG]), ALU.add))
                chain(dve.max(top8[:, 1, :], fine[:, :]))
                chain(dve.max_index(idx8[:, 1, :], top8[:, 1, :], fine[:, :]))
                chain(dve.tensor_copy(pick[:, t, :], idx8[:, 1, 0:2]))
                chain(dve.tensor_tensor(r_exp[:, KT + t:KT + t + 1], top8[:, 1, 1:2], top8[:, 1, 0:1], ALU.subtract))
                for k in range(2):
                    chain(dve.tensor_scalar(hot[:, t, k, :], iota[:, :], pick[:, t, k:k + 1], None, ALU.is_equal))
            dve.sem_inc(exp_in, 1)
            dve.tensor_tensor(member[:, :, :], hot[:, :, 0, :], hot[:, :, 1, :], ALU.add).then_inc(member_ready, 1)
            dve.wait_ge(coarse_exp, 1)
            e1 = r_exp[:, KT:KT + TT]
            chain(dve.tensor_reduce(small[:, 0:TT], r_exp[:, 0:KT].rearrange("p (t g) -> p t g", g=NG), AX.X, ALU.add))
            chain(dve.scalar_tensor_tensor(small[:, 4:8], e1, 1.0, small[:, 0:TT], ALU.add, ALU.mult))
            chain(dve.reciprocal(small[:, 8:12], small[:, 4:8]))
            chain(dve.tensor_copy(gates[:, :, 0], small[:, 8:12]))
            chain(dve.tensor_tensor(gates[:, :, 1], small[:, 8:12], e1, ALU.mult))
            dve.wait_ge(rank_done, 1)
            chain(dve.tensor_copy(rank[:, :, :], psum[:, 3, 0:TT * NE].rearrange("p (t e) -> p t e", e=NE)))
            chain(dve.tensor_scalar(count_i[:, :], psum[:, 3, TT * NE:(TT + 1) * NE], float(SLOTS - 1), None, ALU.add))
            chain(dve.tensor_scalar(count_i[:, :], count_i[:, :], 6, None, ALU.logical_shift_right))
            chain(dve.tensor_scalar(over[:, :], count_i[:, :], -1.0, 0.0, ALU.add, ALU.max))
            chain(dve.tensor_tensor_scan(over_end[:, :], ones2[:, 0:NE], over[:, :], 0.0, ALU.mult, ALU.add))
            dve.tensor_scalar(n_items[0:1, 0:1], over_end[0:1, NE - 1:NE], float(NE), None, ALU.add).then_inc(items_ready, 1)
            chain(dve.tensor_tensor(over_from[:, :], over_end[:, :], over[:, :], ALU.subtract))
            hv = hot[:, :, :, :].rearrange("p t k e -> p (t k) e")
            w4 = wide[:, :, :].rearrange("p (t k) e -> p t k e", k=2)
            chain(dve.tensor_tensor(w4, hot[:, :, :, :], rank[:, :, :].unsqueeze(2).broadcast_to([P, TT, 2, NE]), ALU.mult))
            chain(dve.tensor_reduce(per[:, 0, :], wide[:, :, :], AX.X, ALU.add))
            chain(dve.tensor_tensor(wide[:, :, :], hv, over_from[:, :].unsqueeze(1).broadcast_to([P, 2 * TT, NE]), ALU.mult))
            chain(dve.tensor_reduce(per[:, 1, :], wide[:, :, :], AX.X, ALU.add))
            e_pick = pick[:, :, :].rearrange("p t k -> p (t k)")
            chain(dve.tensor_copy(per_i[:, 0, :], per[:, 0, :]))
            chain(dve.tensor_scalar(per_i[:, 1, :], per_i[:, 0, :], 6, None, ALU.logical_shift_right))
            chain(dve.tensor_copy(per[:, 2, :], per_i[:, 1, :]))
            chain(dve.scalar_tensor_tensor(per[:, 3, :], per[:, 2, :], -float(SLOTS), per[:, 0, :], ALU.mult, ALU.add))
            chain(dve.tensor_scalar(per[:, 4, :], per[:, 2, :], 0.0, None, ALU.is_equal))
            chain(dve.scalar_tensor_tensor(per[:, 5, :], per[:, 1, :], float(NE - 1), per[:, 2, :], ALU.add, ALU.add))
            chain(dve.tensor_tensor(per[:, 6, :], e_pick, per[:, 5, :], ALU.subtract))
            chain(dve.tensor_tensor(per[:, 6, :], per[:, 6, :], per[:, 4, :], ALU.mult))
            chain(dve.tensor_tensor(per[:, 6, :], per[:, 6, :], per[:, 5, :], ALU.add))
            chain(dve.tensor_scalar(per[:, 6, :], per[:, 6, :], 1.0, None, ALU.add))
            chain(dve.scalar_tensor_tensor(slot_i[:, :], per[:, 3, :], float(TABLE), per[:, 6, :], ALU.mult, ALU.add))
            ev = entry[:, :, :].rearrange("p (t k) c -> p t k c", k=2)
            for k in range(2):
                chain(dve.tensor_scalar(ev[:, :, k, 0], twice[:, :], 0.5, None, ALU.mult))
                chain(dve.tensor_scalar(ev[:, :, k, 1], twice[:, :], float(k), None, ALU.add))
            dve.sem_inc(entries_ready, 1)
            dve.wait_ge(which_in, 16)
            wv = which[:, :].rearrange("p (j e) -> p j e", e=NE)
            chain(dve.tensor_tensor(which_o[:, :, :], over_end[0:1, :].unsqueeze(1).broadcast_to([1, MAX_ITEMS - NE, NE]), wv, ALU.is_le))
            chain(dve.tensor_reduce(extra_f[:, :], which_o[:, :, :], AX.X, ALU.add))
            dve.tensor_scalar(extra_e[:, :], extra_f[:, :], float(NE - 1), None, ALU.min).then_inc(items_ready, 1)

            dve.wait_ge(items_ready, 2)
            items = dve.value_load(n_items[0:1, 0:1], min_val=NE, max_val=MAX_ITEMS)
            dve.sem_inc(y_ready, 1)

            def split_x(half, n):
                dve.wait_ge(xT_rounded, n + 1)
                ks = slice(8 * half, 8 * half + 8)
                dve.tensor_tensor(xT[:, ks, 1, :], psum[:, 6, :].rearrange("p (k s) -> p k s", s=SLOTS), xT[:, ks, 0, :].bitcast(F32),
                                  ALU.subtract).then_inc(xT_split, 1)

            split_x(0, 0)
            split_x(1, 1)
            links += chain.n

            def add_y(i):
                dve.wait_ge(y_low_out, i + 1)
                dve.wait_ge(y_free, i + 1)
                dve.tensor_tensor(y_sb[:, :].rearrange("p (b n) -> p b n", b=4), psum[0:SLOTS, 0:4, :],
                                  y_low[:, :].rearrange("p (b n) -> p b n", b=4), ALU.add).then_inc(y_ready, 1)

            with dve.Fori(0, items) as i:
                body = Chain(dve, dve_chain, links + 3 * i)
                for c in range(ITEM_PIECES):
                    dve.wait_ge(m_rounded, ITEM_PIECES * i + c + 1)
                    dve.tensor_tensor(m_lo[:, c % SPL, :], m_raw[:, c % RAW, :], m_hi[:, c % SPL, :].bitcast(F32),
                                      ALU.subtract).then_inc(m_split, 1)
                    if c == Y_AFTER:
                        add_y(i)
                    if c == UV_AFTER:
                        split_x(0, 2 * i + 2)
                    if c == SILU_AFTER:
                        dve.wait_ge(sig_exp, i + 1)
                        u_v = psum[:, 7, :].rearrange("p (w f s) -> p w f s", w=2, s=SLOTS)
                        body(dve.tensor_scalar(sig[:, :, :], sig[:, :, :], 1.0, None, ALU.add))
                        body(dve.reciprocal(sig[:, :, :], sig[:, :, :]))
                        body(dve.tensor_tensor(sig[:, :, :], sig[:, :, :], u_v[:, 0, :, :], ALU.mult))
                        dve.tensor_tensor(aT32[:, :, :], sig[:, :, :], u_v[:, 1, :, :], ALU.mult).then_inc(a_ready, 1)
                        split_x(1, 2 * i + 3)
                    if c == A_AFTER:
                        dve.wait_ge(a_rounded, i + 1)
                        dve.tensor_tensor(aT[:, :, 1, :], aT32[:, :, :], aT[:, :, 0, :].bitcast(F32), ALU.subtract).then_inc(a_split, 1)
            add_y(items)
            done = Chain(dve, dve_chain, links + 3 * items)
            dve.wait_ge(g2_in, 16)
            for t in range(TT):
                f = fin[:, t % 2, :]
                dve.wait_ge(y0_scaled, t + 1)
                done(dve.scalar_tensor_tensor(f, y_in[:, t % 2, 1, :], gates[:, t, 1:2], f, ALU.mult, ALU.add))
                done(dve.tensor_tensor(f, f, g2_row[:, :], ALU.mult))
                dve.tensor_tensor(f, f, x1[:, t, :], ALU.add).then_inc(fin_ready, 1)

        @block.tensor
        def _(pe):
            mm = pe.matmul
            pe.wait_ge(consts_in, 16 * HEAD_CONSTS)
            mm(psum[:, 0, 0:P], vec_rows[:, :], ident[:, :], is_transpose=True, start=True, stop=True)
            mm(psum[:, 1, 0:10], head_rows[:, :], ident[0:10, 0:10], is_transpose=True, start=True, stop=True).then_inc(vec_done, 1)
            pe.wait_ge(vec_out, 1)
            pe.wait_ge(consts_set, 3)
            pe.sem_inc(ada0_sum, 2)
            with pe.Fori(0, ADA0_GROUPS // 2) as m2:
                for a in range(2):
                    pe.wait_ge(x_normed, 2 * m2 + a + 1)
                    for q in range(4):
                        pe.wait_ge(xt_out, 8 * m2 + 4 * a + q + 1)
                        for j in range(4):
                            m = pe.transpose(psum[:, q, P * j:P * (j + 1)], x_st[:, a, P * (4 * q + j):P * (4 * q + j + 1)], ident[:, :])
                        m.then_inc(xt_done, 1)
                    pe.wait_ge(ada0_used, 2 * ADA0_RING + 2 * KT * m2 + KT * (a + 1))
                    for j in range(8):
                        m = mm(psum[:, bass.ds(4 + 2 * m2 + a, 1), j:j + 1], ada0_acc[:, a, P * j:P * (j + 1)], ones[:, :], start=True, stop=True)
                    m.then_inc(ada0_sum, 1)
            pe.wait_ge(f_split, 1)
            for k in range(KT):
                pe.wait_ge(act_split, k + 1)
                for n, (wf, act_part) in enumerate(((f_hi, act_hi), (f_lo, act_hi), (f_hi, act_lo))):
                    m = mm(psum[0:NH, 4, :], wf[:, k, :], act_part[:, k, :], start=k == 0 and n == 0, stop=k == KT - 1 and n == 2)
            m.then_inc(f_done, 1)

            def project(k, z, w0, c, free):
                if k % 2 == 0:
                    pe.wait_ge(w_split, WRING + w0 + c + 1)
                half = slice(COLS * (k % 2), COLS * (k % 2 + 1))
                wh, wl = w_hi[:, c % WRING, half], w_lo[:, c % WRING, half]
                for t in range(TT):
                    if k == 0:
                        free(t)
                    tok = slice(P * t, P * (t + 1))
                    mm(psum[:, t, :], act_hi[:, k, tok], wh, start=k == 0, stop=False)
                    mm(psum[:, t, :], act_hi[:, k, tok], wl, start=False, stop=False)
                    m = mm(psum[:, t, :], act_lo[:, k, tok], wh, start=False, stop=k == KT - 1)
                    if k == KT - 1 and t < TT - 1:
                        m.then_inc(z_done, 1)
                if k % 2:
                    m.then_inc(w_used, 1)

            def transpose_heads(n, h, src):
                pe.wait_ge(tr_out, n + 1)
                for t in range(TT):
                    m = pe.transpose(psum[:, 6 + h % 2, P * t:P * (t + 1)], src(t), ident[:, :])
                m.then_inc(tr_done, 1)

            def sum_groups(group, bank):
                pe.wait_ge(ada_used, 2 + KT * (group + 1))
                for j in range(8):
                    m = mm(psum[:, bank, j:j + 1], ada_acc[:, P * j:P * (j + 1)], ones[:, :], start=True, stop=True)
                m.then_inc(ada_sum, 1)

            def attention_scores(p, g):
                for u in (2 * p, 2 * p + 1):
                    h, i = u // TT, u % TT
                    n = P * (i + 1)
                    pe.wait_ge(s_exp, UNITS * g + u + 1)
                    o = psum[:, 4 + u % 2, 0:n]
                    mm(o, qT[:, h, P * i:P * (i + 1)], kT[:, h, 0:n], start=True, stop=False)
                    mm(o, head_sel[:, P * h:P * (h + 1)], neg_cum[:, 0:n], start=False, stop=False)
                    mm(psum[:, 4 + u % 2, P * i:n], ident[:, :], causal[:, :], start=False, stop=True).then_inc(s_done, 1)

            def attention_transpose(p, g):
                for u in (2 * p, 2 * p + 1):
                    pe.wait_ge(p_normed, UNITS * g + u + 1)
                    pe.wait_ge(pt_out, UNITS * g + u + 1)
                    for j in range(u % TT + 1):
                        m = pe.transpose(psum[:, 6 + u % 2, P * j:P * (j + 1)], probs[:, u % 2, P * j:P * (j + 1)], ident[:, :])
                    m.then_inc(pt_done, 1)

            pe.wait_ge(cum_ready, 1)
            pe.sem_inc(w_used, WRING)
            pe.sem_inc(pt_done, 2)
            with pe.Fori(0, GROUPS) as g:
                for c in range(FOX_W):
                    z = FOX_CHUNKS * g + c // WC

                    def free(t):
                        pe.wait_ge(z_out, TT * z + t + 1)

                    for k in (2 * (c % WC), 2 * (c % WC) + 1):
                        step = KT * (c // WC) + k
                        project(k, z, FOX_W * g, c, free)
                        if step == 23:
                            pe.wait_ge(o_out, 1 + HG * g)
                            sum_groups(ADA_GROUPS * g, 5)
                        if 24 <= step <= 30 and step % 2 == 0:
                            h = (step - 24) // 2
                            if h == 0:
                                pe.wait_ge(z_normed, 2 * g + 1)
                            transpose_heads(8 * g + h, h, lambda t: zst[:, t, HD * h:HD * (h + 1)])
                        if 36 <= step <= 39:
                            h = step - 36
                            if h == 0:
                                pe.wait_ge(z_normed, 2 * g + 2)
                            transpose_heads(8 * g + HG + h, h, lambda t: zst[:, t, HD * h:HD * (h + 1)])
                        if step == 39:
                            pe.wait_ge(tr_out, 2 + 8 * g + 8)
                        if step >= 40:
                            p = step - 40
                            if p == 0:
                                pe.wait_ge(sel_ready, g + 1)
                            attention_scores(p, g)
                            if p > 0:
                                attention_transpose(p - 1, g)
                attention_transpose(UNITS // 2 - 1, g)
                pe.wait_ge(z_out, TT + TT * FOX_CHUNKS * (g + 1))
                pe.wait_ge(pt_out, 2 + UNITS * (g + 1))
                sum_groups(ADA_GROUPS * g + 1, 0)
                for h in range(HG):
                    for i in range(TT):
                        start = (0, 1, 3, 6)[i]
                        for j in range(i + 1):
                            m = mm(psum[:, 4 + h, P * i:P * (i + 1)], v_sb[:, j, HD * h:HD * (h + 1)],
                                   pT[:, h, P * (start + j):P * (start + j + 1)], start=j == 0, stop=j == i)
                    m.then_inc(pv_done, 1)
                pe.wait_ge(ada_taken, ADA_GROUPS * (g + 1))
            pe.wait_ge(o_out, 1 + HG * GROUPS)
            with pe.Fori(0, GROUPS) as g:
                for c in range(RET_W):
                    z = Z_RET + RET_CHUNKS * g + c // WC

                    def free(t):
                        pe.wait_ge(z_out, TT * z + t + 1)

                    for k in (2 * (c % WC), 2 * (c % WC) + 1):
                        step = KT * (c // WC) + k
                        project(k, z, GROUPS * FOX_W + RET_W * g, c, free)
                        if 24 <= step <= 30 and step % 2 == 0:
                            h = (step - 24) // 2
                            if h == 0:
                                pe.wait_ge(z_normed, 4 + 2 * g + 1)
                            transpose_heads(16 + 8 * g + h, h, lambda t: rot[:, t, h, :, :].rearrange("p c d -> p (c d)"))
                        if step == 31:
                            sum_groups(ADA_GROUPS * (GROUPS + g), 5)
                        if 36 <= step <= 39:
                            h = step - 36
                            if h == 0:
                                pe.wait_ge(z_normed, 4 + 2 * g + 2)
                            transpose_heads(16 + 8 * g + HG + h, h, lambda t: rot[:, t, h, :, :].rearrange("p c d -> p (c d)"))
                        if step == 39:
                            pe.wait_ge(tr_out, 2 + 16 + 8 * g + 8)
                        if 40 <= step <= 47:
                            for u in (2 * (step - 40), 2 * (step - 40) + 1):
                                h, j = u // TT, u % TT
                                pe.wait_ge(st_out, UNITS * g + u + 1)
                                mm(psum[:, 4 + u % 2, 0:S - P * j], kT[:, h, P * j:P * (j + 1)], qT[:, h, P * j:S],
                                   start=True, stop=True).then_inc(st_done, 1)
                        if 52 <= step <= 58 and step % 2 == 0:
                            h = (step - 52) // 2
                            if h == 0:
                                pe.wait_ge(z_out, TT + TT * (Z_RET + RET_CHUNKS * g + 3))
                            pe.wait_ge(st_out, 2 + UNITS * g + TT * (h + 1))
                            pe.wait_ge(rv_out, HG * g + h + 1)
                            for i in range(TT):
                                for j in range(i + 1):
                                    start = (0, 512, 896, 1152)[j] + P * (i - j)
                                    m = mm(psum[:, 6 + h % 2, P * i:P * (i + 1)], pT[:, h, start:start + P],
                                           v_sb[:, j, HD * h:HD * (h + 1)], start=j == 0, stop=j == i)
                            m.then_inc(rv_done, 1)
                pe.wait_ge(z_out, TT + TT * (Z_RET + RET_CHUNKS * g + 3) + 1)
                sum_groups(ADA_GROUPS * (GROUPS + g) + 1, 0)
                pe.wait_ge(rv_out, 2 + HG * (g + 1))
                for n in range(2):
                    pe.wait_ge(o_gated, 2 * g + n + 1)
                    for h in range(HG):
                        for t in (2 * n, 2 * n + 1):
                            m = pe.transpose(psum[:, 4 + h, P * t:P * (t + 1)], o_sb[:, h, t, :], ident[:, :])
                        if n == 1:
                            m.then_inc(ot_done, 1)
                pe.wait_ge(ot_out, HG * g + HG)
            pe.wait_ge(mod_ready, 1)
            pe.transpose(psum[0:64, 5, 0:P], mod_cols[:, 32:96], ident[:, :]).then_inc(modT_done, 1)
            pe.wait_ge(z_out, TT + TT * Z_OUT)
            w_first = GROUPS * (FOX_W + RET_W)
            with pe.Fori(0, N_OUT // 2) as m2:
                for c in range(2 * WC):
                    n = 2 * m2 + c // WC

                    def free(t):
                        pe.wait_ge(mix_out, TT * n + t + 1)

                    for k in (2 * (c % WC), 2 * (c % WC) + 1):
                        pe.wait_ge(act_split, KT + k + 1)
                        project(k, Z_OUT + n, w_first + 2 * WC * m2, c, free)
            pe.wait_ge(mix_out, TT + TT * N_OUT)
            for t in range(TT):
                pe.wait_ge(h2_ready, t + 1)
                for q in range(4):
                    if t > 0:
                        pe.wait_ge(h2T_out, 4 * (t - 1) + q + 1)
                    for j in range(4):
                        m = pe.transpose(psum[:, q, P * j:P * (j + 1)], h2[:, t % 2, P * (4 * q + j):P * (4 * q + j + 1)], ident[:, :])
                    m.then_inc(h2T_done, 1)
                if t == 0:
                    pe.wait_ge(route_in, 16 * ROUTE_CONSTS)
                pe.wait_ge(h2T_out, 4 * (t + 1))
                for k in range(KT):
                    m = mm(psum[:, 4 + t, 0:NG + NE], h2T[:, k, :], route_w[:, k, :], start=k == 0, stop=k == KT - 1)
                m.then_inc(logit_done, 1)
            pe.wait_ge(member_ready, 1)
            pe.wait_ge(consts_set, 4)
            for t in range(TT):
                for t2 in range(t + 1):
                    mm(psum[:, 3, NE * t:NE * (t + 1)], strict[:, :] if t2 == t else ones2[:, :], member[:, t2, :],
                       start=t2 == 0, stop=t2 == t)
            for t in range(TT):
                m = mm(psum[:, 3, NE * TT:NE * (TT + 1)], ones2[:, :], member[:, t, :], start=t == 0, stop=t == TT - 1)
            m.then_inc(rank_done, 1)

            def transpose_rows(half, n):
                if n is not None:
                    hold(pe, xT_split, n)
                for j in range(8):
                    k = 8 * half + j
                    m = pe.transpose(psum[:, 6, SLOTS * j:SLOTS * (j + 1)], xg[:, P * k:P * (k + 1)], ident[0:SLOTS, 0:SLOTS])
                m.then_inc(xgT_done, 1)

            pe.wait_ge(items_ready, 2)
            items = pe.value_load(n_items[0:1, 0:1], min_val=NE, max_val=MAX_ITEMS)
            pe.sem_inc(m_used, SPL)
            pe.wait_ge(xg_in, 16)
            transpose_rows(0, None)
            transpose_rows(1, 1)
            with pe.Fori(0, items) as i:
                pe.wait_ge(xT_split, 2 * i + 2)
                pe.wait_ge(uv_out, i + 1)
                for c in range(8):
                    pe.wait_ge(m_split, RAW + ITEM_PIECES * i + c + 1)
                    for j in range(4):
                        k = 4 * (c // 2) + j
                        x_both = xT[:, k, :, :].rearrange("p c s -> p (c s)")
                        for part in (m_hi, m_lo):
                            m = mm(psum[:, 4 + c % 2, :], x_both, part[:, c % SPL, DE * j:DE * (j + 1)],
                                   start=k == 0 and part is m_hi, stop=k == KT - 1 and part is m_lo)
                    m.then_inc(m_used, 1)
                pe.wait_ge(xg_in, 16 * i + 32)
                transpose_rows(0, 2 * i + 2)
                pe.wait_ge(uv_out, i + 2)
                for w in range(2):
                    for f in range(FT):
                        m = mm(psum[:, 7, SLOTS * (FT * w + f):SLOTS * (FT * w + f + 1)], uv_sb[:, w, P * f:P * (f + 1)], pair[:, :],
                               start=True, stop=True)
                m.then_inc(uvT_done, 1)
                transpose_rows(1, 2 * i + 3)
                pe.wait_ge(a_split, i + 1)
                pe.wait_ge(y_ready, i + 2)
                for c in range(8, ITEM_PIECES):
                    f = c - 8
                    pe.wait_ge(m_split, RAW + ITEM_PIECES * i + c + 1)
                    a_both = aT[:, f, :, :].rearrange("p c s -> p (c s)")
                    for part in (m_hi, m_lo):
                        for b in range(4):
                            m = mm(psum[:, b, :], a_both, part[:, c % SPL, DE * b:DE * (b + 1)],
                                   start=f == 0 and part is m_hi, stop=f == FT - 1 and part is m_lo)
                    m.then_inc(m_used, 1)


_INS = ["x", "c", "w_ada", "b_ada", "norm1_w", "w_in", "forget_bias", "q_norm_w", "k_norm_w", "ret_norm_w", "w_out",
        "norm2_w", "w_coarse", "b_coarse", "w_fine", "b_fine", "w1", "w3", "w2"]


def kernel(**inputs):
    import concourse.bacc as bacc
    from concourse.bass_utils import run_bass_kernel_spmd

    nc = bacc.Bacc("TRN2", target_bir_lowering=False, num_devices=1)
    arrays, A = {}, {}
    for name, a in [(n, inputs[n]) for n in _INS] + list(constants().items()):
        a = np.ascontiguousarray(a)
        arrays[f"in_{name}"] = a
        A[name] = nc.dram_tensor(f"in_{name}", a.shape, mybir.dt.from_np(a.dtype), kind="ExternalInput").ap()
    out = nc.dram_tensor("out", (1, S, D), F32, kind="ExternalOutput").ap()
    hybrid_block(nc, A, out)
    r = run_bass_kernel_spmd(nc, [arrays], core_ids=[0])
    return r.results[0]["out"]
```

```python
from contextlib import ExitStack

import numpy as np

import concourse.bass as bass
from concourse import mybir
from concourse.alu_op_type import AluOpType as ALU

F32 = mybir.dt.float32
F32R = mybir.dt.float32r
I32 = mybir.dt.int32
U32 = mybir.dt.uint32
ACT = mybir.ActivationFunctionType
AX = mybir.AxisListType

P = 128
D = 2048
S = 512
HD = 128
NH = 8
KT = D // P
TT = S // P
COLS = 512
HG = COLS // HD
D_IN = 3 * 1024 + NH + 4 * 1024
NG, EPG = 4, 8
NE = NG * EPG
DE = 512
FT = DE // P
EPS = 1e-6
BIG = 1.0e30

FOX_CHUNKS, RET_CHUNKS, GROUPS = 3, 4, 2
FOX_COL = (1024, 0, 2048)
FORGET_COL = 3072
RET_COL = (3080, 4104, 5128, 6152)
WC = KT // 2
WRING = 4
FOX_W, RET_W = FOX_CHUNKS * WC, RET_CHUNKS * WC
Z_RET = GROUPS * FOX_CHUNKS
Z_OUT = Z_RET + GROUPS * RET_CHUNKS
N_OUT = D // COLS
ADA = 1024
ADA0_GROUPS = 2 * D // ADA
ADA0_RING = 4
ADA_GROUPS = 2
ADA_BODY = ADA_GROUPS * KT
UNITS = HG * TT

SLOTS = 64
MAX_ITEMS = NE + (2 * S - 1) // SLOTS + 1
ITEM_PIECES = 12
RAW = 6
SPL = 4
AHEAD = SPL
UV_AFTER, SILU_AFTER, A_AFTER, Y_AFTER = 8, 9, 10, ITEM_PIECES + 1
NOWHERE = 8191
TABLE = MAX_ITEMS + 1


def constants():
    half = HD // 2
    theta = np.float32(10000.0) ** (-np.arange(half, dtype=np.float32) / np.float32(half))
    ang = np.arange(S, dtype=np.float32)[:, None] * theta[None, :]
    rot = np.stack([np.cos(ang), np.sin(ang)], 1).astype(np.float32)
    rot = rot.reshape(TT, P, 2, half).transpose(1, 2, 0, 3)
    g = 1.0 - 2.0 ** (-5.0 - np.arange(NH))
    diff = np.arange(S)[None, :] - np.arange(P)[:, None]
    decay = np.where(diff >= 0, g[:, None, None] ** np.maximum(diff, 0)[None], 0.0) * HD ** -0.5
    upper = np.triu(np.ones((P, P), np.float32))
    pair = np.concatenate([np.eye(SLOTS), np.eye(SLOTS)]).astype(np.float32)
    one_head = np.zeros((NH, NH, P), np.float32)
    for h in range(NH):
        one_head[h, h] = 1.0
    iota = np.broadcast_to(np.arange(SLOTS, dtype=np.float32), (P, SLOTS))
    token = np.arange(TT)[None, :, None] * P + np.arange(P)[:, None, None] + np.zeros((1, 1, 2), int)
    entry = np.stack([token, 2 * token + np.arange(2)[None, None, :]], 1) - NOWHERE
    c = {
        "ident": np.eye(P, dtype=np.float32),
        "rot": np.ascontiguousarray(rot),
        "decay": decay.astype(np.float32),
        "causal": np.where(upper.T > 0, 0.0, -BIG).astype(np.float32),
        "strict": upper - np.eye(P, dtype=np.float32),
        "pair": pair,
        "one_head": one_head.reshape(NH, NH * P),
        "iota": np.ascontiguousarray(iota),
        "entry": entry.reshape(P, 2, 2 * TT).astype(np.float32),
    }
    return {k: np.ascontiguousarray(v) for k, v in c.items()}


class Chain:

    def __init__(self, eng, sem, base):
        self.eng, self.sem, self.base, self.n = eng, sem, base, 0

    def __call__(self, ins):
        self.n += 1
        ins.then_inc(self.sem, 1)
        self.eng.wait_ge(self.sem, self.base + self.n)


def hybrid_block(nc, A, out):
    ctx = ExitStack()
    with ctx:
        size = 212832
        ctx.enter_context(nc.sbuf_tensor("arena", [P, size // 4], F32))
        origin = 16512

        def at(name, shape, dtype, offset):
            n = 4 * int(np.prod(shape[1:]))
            assert offset % 32 == 0 and offset + n <= size, (name, offset, n)
            return nc.alloc_sbuf_tensor_at(name, shape, dtype, offset=origin + offset)

        def dram(name, shape, dtype=F32):
            return nc.dram_tensor(name, shape, dtype, kind="Internal").ap()

        def sem(name):
            return ctx.enter_context(nc.semaphore(name))

        psum = ctx.enter_context(nc.psum_tensor("psum", [P, 8, 512], F32))

        w_raw = at("w_raw", [P, WRING, 2 * COLS], F32, 0)
        w_hi = at("w_hi", [P, WRING, 2 * COLS], F32R, 16384)
        w_lo = at("w_lo", [P, WRING, 2 * COLS], F32R, 32768)
        ada_raw = at("ada_raw", [P, 2, ADA], F32, 49152)
        ada_acc = at("ada_acc", [P, ADA], F32, 57344)
        act_hi = at("act_hi", [P, KT, S], F32R, 61440)
        act_lo = at("act_lo", [P, KT, S], F32R, 94208)
        act32 = at("act32", [P, KT, S], F32, 94208)
        square_out = at("square_out", [P, D], F32, 61440)
        C0 = 126976
        ident = at("ident", [P, P], F32, C0)
        rot_tab = at("rot_tab", [P, 2, TT, HD // 2], F32, C0 + 512)
        vec_cols = at("vec_cols", [P, P], F32, C0 + 2560)
        mod_cols = at("mod_cols", [P, 96], F32, C0 + 3072)
        head_cols = at("head_cols", [P, 10], F32, C0 + 3456)
        ones = at("ones", [P, 1], F32, C0 + 3520)
        c_cols = at("c_cols", [P, KT], F32, C0 + 3552)
        minus_half = at("minus_half", [P, KT], F32, C0 + 3616)
        ssq = at("ssq", [P, KT], F32, C0 + 3680)
        rstd = at("rstd", [P, KT], F32, C0 + 3744)
        row_max = at("row_max", [P, 2], F32, C0 + 3808)
        row_sum = at("row_sum", [P, 2], F32, C0 + 3840)
        row_inv = at("row_inv", [P, 2], F32, C0 + 3872)
        mod_sum = at("mod_sum", [P, ADA // P], F32, C0 + 3904)
        assert C0 + 3936 <= 130912
        B0 = 130912
        x1 = at("x1", [P, TT, D], F32, B0)
        zst = at("zst", [P, TT, COLS], F32, B0)
        qT = at("qT", [P, HG, S], F32, B0 + 8192)
        kT = at("kT", [P, HG, S], F32, B0 + 16384)
        v_sb = at("v_sb", [P, TT, COLS], F32, B0 + 24576)
        pT = at("pT", [P, HG, 10 * P], F32, B0 + 32768)
        probs = at("probs", [P, 2, S], F32, B0 + 53248)
        one_head = at("one_head", [NH, NH * P], F32, B0 + 57344)
        neg_cum = at("neg_cum", [NH, S], F32, B0 + 61440)
        head_sel = at("head_sel", [NH, HG * P], F32, B0 + 63488)
        causal = at("causal", [P, P], F32, B0 + 65536)
        f_raw = at("f_raw", [P, KT, NH], F32, B0 + 66048)
        f_hi = at("f_hi", [P, KT, NH], F32R, B0 + 66560)
        f_lo = at("f_lo", [P, KT, NH], F32R, B0 + 67072)
        f_bias = at("f_bias", [NH, 1], F32, B0 + 67584)
        f_y = at("f_y", [NH, S], F32, B0 + 69632)
        f_e = at("f_e", [NH, S], F32, B0 + 71680)
        f_ones = at("f_ones", [NH, S], F32, B0 + 73728)
        rot = at("rot", [P, TT, HG, 2, HD // 2], F32, B0 + 61440)
        o_sb = at("o_sb", [P, HG, TT, HD], F32, B0 + 61440)
        decay = at("decay", [P, 2, S], F32, B0 + 69632)
        sq = at("sq", [P, COLS], F32, B0 + 77824)
        o_stage = at("o_stage", [P, HG, S], F32, B0 + 69632)
        o_back = at("o_back", [P, 10, S], F32, B0 + 32768)
        o_back2 = at("o_back2", [P, 2, S], F32, B0 + 73728)
        ret_out = at("ret_out", [P, HG, S], F32, B0 + 16384)
        ada0_raw = at("ada0_raw", [P, ADA0_RING, 2 * ADA], F32, B0)
        ada0_acc = at("ada0_acc", [P, 2, ADA], F32, B0 + 32768)
        x_st = at("x_st", [P, 2, D], F32, B0 + 49152)
        vec_rows = at("vec_rows", [P, P], F32, B0 + 69632)
        head_rows = at("head_rows", [10, P], F32, B0 + 70144)
        c_tmp = at("c_tmp", [P, KT], F32, B0 + 70656)
        g1_row = at("g1_row", [P, D], F32, 49152)
        mod_rows_sb = at("mod_rows_sb", [64, P], F32, 57344)
        ss2 = at("ss2", [P, TT, N_OUT], F32, 57856)
        R0 = 163680
        m_raw = at("m_raw", [P, RAW, D], F32, R0)
        scale2 = at("scale2", [P, D], F32, R0 + 4 * 8192)
        shift2 = at("shift2", [P, D], F32, R0 + 5 * 8192)
        m_hi = at("m_hi", [P, SPL, D], F32R, 0)
        m_lo = at("m_lo", [P, SPL, D], F32R, 32768)
        pair = at("pair", [P, SLOTS], F32, 65536)
        table = at("table", [SLOTS, 2, TABLE], I32, 65792)
        idx_in = at("idx_in", [SLOTS, 1], I32, 66208)
        idx_out = at("idx_out", [SLOTS, 1], I32, 66240)
        gates = at("gates", [P, TT, 2], F32, 66272)
        extra_e = at("extra_e", [1, MAX_ITEMS - NE], I32, 66304)
        n_items = at("n_items", [1, 1], I32, 66368)
        xg = at("xg", [SLOTS, D], F32, 67584)
        xT = at("xT", [P, KT, 2, SLOTS], F32R, 75776)
        uv_sb = at("uv_sb", [P, 2, DE], F32, 83968)
        aT32 = at("aT32", [P, FT, SLOTS], F32, 88064)
        sig = at("sig", [P, FT, SLOTS], F32, 89088)
        aT = at("aT", [P, FT, 2, SLOTS], F32R, 90112)
        y_low = at("y_low", [SLOTS, D], F32, 92160)
        y_sb = at("y_sb", [SLOTS, D], F32, 100352)
        strict = at("strict", [P, P], F32, C0 + 512)
        ones2 = at("ones2", [P, P], F32, C0 + 1024)
        iota = at("iota", [P, SLOTS], F32, C0 + 1536)
        route_b = at("route_b", [P, NG + NE], F32, C0 + 1792)
        entry = at("entry", [P, 2, 2 * TT], F32, C0 + 1952)
        route_w = at("route_w", [P, KT, NG + NE], F32, 57920)
        h2 = at("h2", [P, 3, D], F32, 67584)
        h2T = at("h2T", [P, 2, KT, P], F32, 94208)
        where = [110592]

        def small_buffer(name, shape, dtype=F32):
            offset = where[0]
            where[0] += (4 * int(np.prod(shape[1:])) + 31) // 32 * 32
            return at(name, shape, dtype, offset)

        logitT = small_buffer("logitT", [NG + NE, 2, P])
        logit = small_buffer("logit", [P, TT, NG + NE])
        coarse8 = small_buffer("coarse8", [P, 8])
        top8 = small_buffer("top8", [P, 2, 8])
        idx8 = small_buffer("idx8", [P, 2, 8], U32)
        pick = small_buffer("pick", [P, TT, 2])
        hot = small_buffer("hot", [P, TT, 2, NE])
        member = small_buffer("member", [P, TT, NE])
        fine = small_buffer("fine", [P, NE])
        small = small_buffer("small", [P, 16])
        count_i = small_buffer("count_i", [P, NE], I32)
        over = small_buffer("over", [P, NE])
        over_end = small_buffer("over_end", [P, NE])
        over_from = small_buffer("over_from", [P, NE])
        wide = small_buffer("wide", [P, TT * 2, NE])
        per = small_buffer("per", [P, 7, TT * 2])
        per_i = small_buffer("per_i", [P, 2, TT * 2], I32)
        slot_hot = small_buffer("slot_hot", [P, 2 * TT, SLOTS])
        column_hot = small_buffer("column_hot", [P, 2 * TT, TABLE])
        entry_hot = small_buffer("entry_hot", [P, 2 * TT, 2, TABLE])
        which_o = small_buffer("which_o", [1, MAX_ITEMS - NE, NE])
        extra_f = small_buffer("extra_f", [1, MAX_ITEMS - NE])
        r_exp = small_buffer("r_exp", [P, KT + TT])
        ms2 = small_buffer("ms2", [P, TT])
        r2 = small_buffer("r2", [P, TT])
        assert where[0] <= C0
        y_in = at("y_in", [P, TT, 2, D], F32, 0)
        g2_row = at("g2_row", [P, D], F32, 67584)
        fin = at("fin", [P, TT, D], F32, 75776)

        o_dram = dram("o_dram", [2 * NH, P, S])
        mod_dram = dram("mod_dram", [64, P])
        h2_dram = dram("h2_dram", [S, D])
        y_dram = dram("y_dram", [2 * S, D])

        x_rows = A["x"].rearrange("a (t p) d -> (a t) p d", p=P)
        out_rows = out.rearrange("a (t p) d -> (a t) p d", p=P)
        w_ada = A["w_ada"].rearrange("l (p k) n -> p (l k) n", k=KT)
        w_in = A["w_in"].rearrange("l (k p) n -> p (l k) n", p=P)
        w_out = A["w_out"].rearrange("l (k p) n -> p (l k) n", p=P)
        w1 = A["w1"].rearrange("l e (p k) n -> (l e) p (k n)", k=KT)
        w3 = A["w3"].rearrange("l e (p k) n -> (l e) p (k n)", k=KT)
        w2 = A["w2"].rearrange("l e (k p) n -> (l e) p k n", p=P)
        mod_flat = mod_dram.rearrange("a b -> (a b)")

        consts_in = sem("consts_in")
        held = sem("held")
        consts_set = sem("consts_set")
        attn_consts_in = sem("attn_consts_in")
        x_in = [sem(f"x_in{i}") for i in range(2)]
        ada0_in = [sem(f"ada0_in{i}") for i in range(ADA0_RING)]
        c_in = sem("c_in")
        ada0_used = sem("ada0_used")
        ada0_sum = sem("ada0_sum")
        c_exp = sem("c_exp")
        vec_done = sem("vec_done")
        vec_out = sem("vec_out")
        x_square = sem("x_square")
        x_rstd = sem("x_rstd")
        x_normed = sem("x_normed")
        xt_done = sem("xt_done")
        xt_out = sem("xt_out")
        dve_chain = sem("dve_chain")
        act_chain = sem("act_chain")
        pool_chain = sem("pool_chain")
        h_scaled = sem("h_scaled")
        act_rounded = sem("act_rounded")
        act_split = sem("act_split")
        f_in = sem("f_in")
        f_rounded = sem("f_rounded")
        f_split = sem("f_split")
        f_done = sem("f_done")
        f_abs = sem("f_abs")
        f_log = sem("f_log")
        cum_ready = sem("cum_ready")
        w_in_sem = [sem(f"w_in{i}") for i in range(WRING)]
        w_rounded = sem("w_rounded")
        w_split = sem("w_split")
        w_used = sem("w_used")
        ada_in = [sem(f"ada_in{i}") for i in range(2)]
        ada_used = sem("ada_used")
        ada_sum = sem("ada_sum")
        ada_taken = sem("ada_taken")
        z_done = sem("z_done")
        z_out = sem("z_out")
        sq_ready = sem("sq_ready")
        sel_ready = sem("sel_ready")
        rs_ready = sem("rs_ready")
        z_normed = sem("z_normed")
        tr_done = sem("tr_done")
        tr_out = sem("tr_out")
        s_done = sem("s_done")
        s_max = sem("s_max")
        s_exp = sem("s_exp")
        p_normed = sem("p_normed")
        pt_done = sem("pt_done")
        pt_out = sem("pt_out")
        pv_done = sem("pv_done")
        o_out = sem("o_out")
        o_stored = sem("o_stored")
        stage_free = sem("stage_free")
        st_done = sem("st_done")
        st_out = sem("st_out")
        decay_in = [sem(f"decay_in{i}") for i in range(2)]
        decay_used = sem("decay_used")
        rv_done = sem("rv_done")
        rv_out = sem("rv_out")
        gate_out = sem("gate_out")
        gate_log = sem("gate_log")
        gate_exp = sem("gate_exp")
        o_gated = sem("o_gated")
        ot_done = sem("ot_done")
        ot_out = sem("ot_out")
        mod_ready = sem("mod_ready")
        modT_done = sem("modT_done")
        modT_out = sem("modT_out")
        mod_stored = sem("mod_stored")
        o_in = [sem(f"o_in{i}") for i in range(3)]
        x_again = sem("x_again")
        g1_in = sem("g1_in")
        mix_out = sem("mix_out")
        x1_ready = sem("x1_ready")
        x1_square = sem("x1_square")
        r2_ready = sem("r2_ready")
        row2_in = sem("row2_in")
        route_in = sem("route_in")
        pair_in = sem("pair_in")
        h2_ready = sem("h2_ready")
        h2_stored = [sem(f"h2_stored{i}") for i in range(3)]
        ms2_ready = sem("ms2_ready")
        h2T_done = sem("h2T_done")
        h2T_out = sem("h2T_out")
        logit_done = sem("logit_done")
        logitT_done = sem("logitT_done")
        logitT_out = sem("logitT_out")
        logit_taken = sem("logit_taken")
        coarse_exp = sem("coarse_exp")
        exp_in = sem("exp_in")
        member_ready = sem("member_ready")
        rank_done = sem("rank_done")
        items_ready = sem("items_ready")
        entries_hot = sem("entries_hot")
        entries_placed = sem("entries_placed")
        table_ready = sem("table_ready")
        m_in = [sem(f"m_in{i}") for i in range(RAW)]
        m_rounded = sem("m_rounded")
        m_split = sem("m_split")
        m_used = sem("m_used")
        idx_ready = sem("idx_ready")
        xg_in = sem("xg_in")
        xgT_done = sem("xgT_done")
        xT_rounded = sem("xT_rounded")
        xT_split = sem("xT_split")
        uv_out = sem("uv_out")
        uvT_done = sem("uvT_done")
        sig_exp = sem("sig_exp")
        a_ready = sem("a_ready")
        a_rounded = sem("a_rounded")
        a_split = sem("a_split")
        y_low_out = sem("y_low_out")
        y_ready = sem("y_ready")
        y_scattered = sem("y_scattered")
        y_free = sem("y_free")
        y_back = [sem(f"y_back{i}") for i in range(TT)]
        g2_in = sem("g2_in")
        y0_scaled = sem("y0_scaled")
        fin_ready = sem("fin_ready")
        fin_stored = sem("fin_stored")

        block = ctx.enter_context(nc.Block())

        HEAD_CONSTS = 8
        ATTN_CONSTS = 3
        ROUTE_CONSTS = 10

        def extra_pieces(c):
            return 2 if c % 3 == 2 else 1

        def hold(eng, semaphore, value):
            eng.wait_ge(semaphore, value)
            eng.sem_inc(held, 1)

        def wait_z(eng, z, t):
            if t < TT - 1:
                eng.wait_ge(z_done, (TT - 1) * z + t + 1)
            else:
                eng.wait_ge(w_used, WRING + WC * (z + 1))

        def head_out(k):
            if k < 10:
                return o_back[:, k, :]
            return o_back2[:, k - 10, :] if k < 12 else ret_out[:, k - 12, :]

        @block.sync
        def _(sp):
            with sp.Fori(0, ADA0_GROUPS) as g:
                for n in range(KT // 2):
                    hold(sp, ada0_used, KT * g + 2 * n + 2)
                    sp.dma_start(ada0_raw[:, n % ADA0_RING, :].rearrange("p (k n) -> p k n", k=2),
                                 w_ada[:, 2 * n:2 * n + 2, bass.ds(ADA * g, ADA)]).then_inc(ada0_in[n % ADA0_RING], 16)

            def load_w(src, col, c, w0):
                hold(sp, w_split, w0 + c + 1)
                k = 2 * (c % WC)
                sp.dma_start(w_raw[:, c % WRING, :].rearrange("p (k n) -> p k n", k=2),
                             src[:, k:k + 2, bass.ds(col, COLS)]).then_inc(w_in_sem[c % WRING], 16)

            def load_ada(j, a0, group0):
                hold(sp, ada_used, a0 + j + 1)
                sp.dma_start(ada_raw[:, j % 2, :],
                             w_ada[:, j % KT, bass.ds(2 * D + ADA * (group0 + j // KT), ADA)]).then_inc(ada_in[j % 2], 16)

            with sp.Fori(0, GROUPS) as g:
                j = 0
                for c in range(FOX_W):
                    load_w(w_in, FOX_COL[c // WC] + COLS * g, c, FOX_W * g)
                    for _ in range(extra_pieces(c)):
                        load_ada(j, ADA_BODY * g, ADA_GROUPS * g)
                        j += 1
            with sp.Fori(0, GROUPS) as g:
                for c in range(RET_W):
                    load_w(w_in, RET_COL[c // WC] + COLS * g, c, GROUPS * FOX_W + RET_W * g)
                    load_ada(c, ADA_BODY * (GROUPS + g), ADA_GROUPS * (GROUPS + g))
            sp.wait_ge(rv_done, HG * GROUPS)
            sp.wait_ge(o_stored, 16 * (GROUPS + 1))
            for n in range(2):
                sp.dma_start(o_back[:, 5 * n:5 * n + 5, :], o_dram[5 * n:5 * n + 5].rearrange("k p s -> p k s")).then_inc(o_in[n], 16)
            sp.dma_start(o_back2[:, :, :], o_dram[10:12].rearrange("k p s -> p k s")).then_inc(o_in[2], 16)
            w_first = GROUPS * (FOX_W + RET_W)
            with sp.Fori(0, N_OUT) as n:
                for c in range(WC):
                    load_w(w_out, COLS * n, c, w_first + WC * n)

            def load_item(i, e, pieces=ITEM_PIECES):
                for c in range(pieces):
                    hold(sp, m_split, ITEM_PIECES * i + c + 1)
                    if c < 8:
                        src = (w1, w3)[c % 2][e, :, 4 * DE * (c // 2):4 * DE * (c // 2 + 1)]
                    else:
                        src = w2[e, :, c - 8, :]
                    sp.dma_start(m_raw[:, c % RAW, :], src).then_inc(m_in[c % RAW], 16)

            sp.wait_ge(act_split, 2 * KT)
            with sp.Fori(0, NE) as i:
                load_item(i, i)
            sp.wait_ge(items_ready, 2)
            items = sp.value_load(n_items[0:1, 0:1], min_val=NE, max_val=MAX_ITEMS)
            with sp.If(items > NE):
                with sp.Fori(NE, items) as i:
                    e = sp.value_load(extra_e[0:1, bass.ds(i - NE, 1)], min_val=0, max_val=NE - 1)
                    load_item(i, e)
            with sp.Else():
                sp.nop()
            load_item(items, 0, AHEAD)
            hold(sp, xgT_done, 2 * items + 2)
            hold(sp, xg_in, 16 * items + 16)
            sp.dma_start(g2_row[:, :], mod_flat[3 * D:4 * D].partition_broadcast(P)).then_inc(g2_in, 16)
            hold(sp, m_split, RAW + ITEM_PIECES * items + AHEAD)
            hold(sp, y_scattered, 16 * items)
            y_rows = y_dram.rearrange("(t p k) d -> t p k d", p=P, k=2)
            for t in range(TT):
                sp.dma_start(y_in[:, t, :, :], y_rows[t]).then_inc(y_back[t], 16)
            for t in range(TT):
                sp.wait_ge(fin_ready, t + 1)
                sp.dma_start(out_rows[t], fin[:, t, :]).then_inc(fin_stored, 16)
            sp.wait_ge(fin_stored, 16 * TT)

        @block.gpsimd
        def _(pool):
            chain = Chain(pool, pool_chain, 0)
            pool.memset(ones[:, :], 1.0).then_inc(consts_set, 1)
            pool.memset(minus_half[:, :], -0.5).then_inc(consts_set, 1)
            pool.memset(f_ones[:, :], 1.0).then_inc(consts_set, 1)
            pool.dma_start(c_cols[:, :], A["c"].rearrange("a (p k) -> (a p) k", k=KT)).then_inc(c_in, 16)
            for t in range(2):
                pool.dma_start(x_st[:, t, :], x_rows[t]).then_inc(x_in[t], 16)
            pool.dma_start(ident[:, :], A["ident"]).then_inc(consts_in, 16)
            pool.dma_start(rot_tab[:, :, :, :], A["rot"]).then_inc(consts_in, 16)
            pool.dma_start(vec_rows[0:96, :], A["b_ada"].rearrange("l (r p) -> (l r) p", p=P)).then_inc(consts_in, 16)
            pool.dma_start(vec_rows[96:112, :], A["norm1_w"].rearrange("l (r p) -> (l r) p", p=P)).then_inc(consts_in, 16)
            pool.dma_start(vec_rows[112:128, :], A["norm2_w"].rearrange("l (r p) -> (l r) p", p=P)).then_inc(consts_in, 16)
            pool.dma_start(head_rows[0:1, :], A["q_norm_w"]).then_inc(consts_in, 16)
            pool.dma_start(head_rows[1:2, :], A["k_norm_w"]).then_inc(consts_in, 16)
            pool.dma_start(head_rows[2:10, :], A["ret_norm_w"].rearrange("l (r p) -> (l r) p", p=P)).then_inc(consts_in, 16)
            with nc.allow_non_contiguous_dma("eight columns"):
                pool.dma_start(f_raw[:, :, :], w_in[:, :, FORGET_COL:FORGET_COL + NH]).then_inc(f_in, 16)
            pool.dma_start(causal[:, :], A["causal"]).then_inc(attn_consts_in, 16)
            pool.dma_start(f_bias[:, :], A["forget_bias"].rearrange("l h -> h l")).then_inc(attn_consts_in, 16)

            def inverse_root(src, dst, n, count):
                chain(pool.tensor_scalar(dst, src, 1.0 / count, EPS, ALU.mult, ALU.add))
                return pool.tensor_tensor(dst, dst, minus_half[:, 0:n], ALU.pow)

            pool.wait_ge(consts_set, 3)
            for t in range(TT):
                pool.wait_ge(x_square, t + 1)
                inverse_root(ssq[:, t:t + 1], rstd[:, t:t + 1], 1, D).then_inc(x_rstd, 1)
                if t + 2 < TT:
                    pool.wait_ge(xt_done, 4 * (t + 1))
                    pool.dma_start(x_st[:, t % 2, :], x_rows[t + 2]).then_inc(x_in[t % 2], 16)
            pool.wait_ge(xt_done, 4 * TT)
            pool.dma_start(one_head[:, :], A["one_head"]).then_inc(attn_consts_in, 16)

            pool.sem_inc(stage_free, 1)
            links = chain.n
            with pool.Fori(0, GROUPS) as g:
                body = Chain(pool, pool_chain, links + 2 * g)
                for n in range(2):
                    hold(pool, sq_ready, 2 * g + n + 1)
                    body(pool.tensor_scalar(rstd[:, :], ssq[:, :], 1.0 / HD, EPS, ALU.mult, ALU.add))
                    pool.tensor_tensor(rstd[:, :], rstd[:, :], minus_half[:, :], ALU.pow).then_inc(rs_ready, 1)
                hold(pool, o_out, 1 + HG * g + HG)
                pool.dma_start(o_dram[bass.ds(HG * g, HG)].rearrange("k p s -> p k s"), o_stage[:, :, :]).then_inc(o_stored, 16)
                hold(pool, o_stored, 16 * (g + 1))
                pool.sem_inc(stage_free, 1)
            links = links + 2 * GROUPS
            pool.wait_ge(o_out, 1 + HG * GROUPS)
            with pool.Fori(0, GROUPS) as g:
                for h in range(HG):
                    hold(pool, decay_used, HG * g + h + 1)
                    pool.dma_start(decay[:, h % 2, :], A["decay"][HG * g + h]).then_inc(decay_in[h % 2], 16)
                body = Chain(pool, pool_chain, links + HG * g)
                for h in range(HG):
                    hold(pool, sq_ready, 2 * GROUPS + HG * g + h + 1)
                    cols = slice(TT * h, TT * (h + 1))
                    body(pool.tensor_scalar(rstd[:, cols], ssq[:, cols], 1.0 / HD, EPS, ALU.mult, ALU.add))
                    pool.tensor_tensor(rstd[:, cols], rstd[:, cols], minus_half[:, 0:TT], ALU.pow).then_inc(rs_ready, 1)
                hold(pool, ot_out, 1 + HG * g + HG)
                pool.dma_start(o_dram[bass.ds(NH + HG * g, HG)].rearrange("k p s -> p k s"), ret_out[:, :, :]).then_inc(o_stored, 16)
            links = links + HG * GROUPS
            chain = Chain(pool, pool_chain, links)
            pool.wait_ge(modT_out, 1)
            pool.dma_start(mod_dram, mod_rows_sb[:, :]).then_inc(mod_stored, 16)
            pool.wait_ge(mod_stored, 16)
            pool.wait_ge(act_split, 2 * KT)
            pool.wait_ge(o_stored, 16 * (GROUPS + GROUPS))
            for t in range(TT):
                pool.dma_start(x1[:, t, :], x_rows[t]).then_inc(x_again, 16)
            pool.dma_start(shift2[:, :], mod_flat[D:2 * D].partition_broadcast(P)).then_inc(row2_in, 16)
            pool.dma_start(scale2[:, :], mod_flat[2 * D:3 * D].partition_broadcast(P)).then_inc(row2_in, 16)
            pool.dma_start(g1_row[:, :], mod_flat[0:D].partition_broadcast(P)).then_inc(g1_in, 16)
            pool.memset(ones2[:, :], 1.0).then_inc(consts_set, 1)
            pool.dma_start(route_w[:, :, 0:NG], A["w_coarse"].rearrange("l (p k) g -> (l p) k g", k=KT)).then_inc(route_in, 16)
            for gr in range(NG):
                pool.dma_start(route_w[:, :, NG + EPG * gr:NG + EPG * (gr + 1)],
                               A["w_fine"][0, gr].rearrange("(p k) e -> p k e", k=KT)).then_inc(route_in, 16)
            pool.dma_start(route_b[:, 0:NG], A["b_coarse"].to_broadcast([P, NG])).then_inc(route_in, 16)
            pool.dma_start(route_b[:, NG:], A["b_fine"].rearrange("l g e -> l (g e)").to_broadcast([P, NE])).then_inc(route_in, 16)
            for table_of, name in ((strict[:, :], "strict"), (iota[:, :], "iota"), (entry[:, :, :], "entry")):
                pool.dma_start(table_of, A[name]).then_inc(route_in, 16)
            pool.wait_ge(ms2_ready, 1)
            chain(pool.tensor_scalar(ms2[:, :], ms2[:, :], 1.0 / D, EPS, ALU.mult, ALU.add))
            pool.tensor_tensor(r2[:, :], ms2[:, :], minus_half[:, 0:TT], ALU.pow).then_inc(r2_ready, 1)
            pool.dma_start(pair[:, :], A["pair"]).then_inc(pair_in, 16)
            for t in range(TT):
                pool.wait_ge(h2_ready, t + 1)
                pool.dma_start(h2_dram[P * t:P * (t + 1), :], h2[:, t % 3, :]).then_inc(h2_stored[t % 3], 16)
            for n in range(3):
                pool.wait_ge(h2_stored[n], 32 if n == 0 else 16)
            pool.wait_ge(h2T_done, 4 * TT)
            pool.memset(xg[:, :], 0.0).then_inc(consts_set, 1)
            pool.wait_ge(table_ready, 1)
            pool.wait_ge(items_ready, 2)
            items = pool.value_load(n_items[0:1, 0:1], min_val=NE, max_val=MAX_ITEMS)
            pool.wait_ge(consts_set, 5)

            def gather():
                pool.indirect_dma_start(out=xg[:, :], out_offset=None, in_=h2_dram,
                                        in_offset=bass.IndirectOffsetOnAxis(ap=idx_in[:, 0:1], axis=0),
                                        bounds_check=S - 1, oob_is_err=False).then_inc(xg_in, 16)

            pool.tensor_copy(idx_in[:, :], table[:, 0, 0:1]).then_inc(idx_ready, 1)
            pool.wait_ge(idx_ready, 1)
            gather()
            pool.sem_inc(y_free, 1)

            with pool.Fori(0, items) as i:
                hold(pool, xgT_done, 2 * i + 2)
                hold(pool, xg_in, 16 * i + 16)
                pool.tensor_copy(idx_in[:, :], table[:, 0, bass.ds(i + 1, 1)]).then_inc(idx_ready, 1)
                hold(pool, idx_ready, 2 * i + 2)
                gather()
                pool.tensor_copy(idx_out[:, :], table[:, 1, bass.ds(i, 1)]).then_inc(idx_ready, 1)
                hold(pool, idx_ready, 2 * i + 3)
                hold(pool, y_ready, i + 2)
                pool.indirect_dma_start(out=y_dram, out_offset=bass.IndirectOffsetOnAxis(ap=idx_out[:, 0:1], axis=0),
                                        in_=y_sb[:, :], in_offset=None,
                                        bounds_check=2 * S - 1, oob_is_err=False).then_inc(y_scattered, 16)
                hold(pool, y_scattered, 16 * i + 16)
                pool.sem_inc(y_free, 1)

        @block.scalar
        def _(act):
            chain = Chain(act, act_chain, 0)
            act.sem_inc(xt_out, 4)
            act.wait_ge(c_in, 16)
            act.activation(c_tmp[:, :], c_cols[:, :], ACT.Exp, scale=-1.0).then_inc(c_exp, 1)
            for t in range(TT):
                act.wait_ge(x_in[t % 2], 16 * (t // 2 + 1))
                if t > 0:
                    act.wait_ge(x_square, t)
                act.activation(square_out[:, :], x_st[:, t % 2, :], ACT.Square, accum_out=ssq[:, t:t + 1]).then_inc(x_square, 1)
                if t > 0:
                    for q in range(4):
                        act.wait_ge(xt_done, 4 * (t - 1) + q + 1)
                        act.activation(act32[:, 4 * q:4 * q + 4, P * (t - 1):P * t],
                                       psum[:, q, :].rearrange("p (k s) -> p k s", k=4), ACT.Copy).then_inc(xt_out, 1)
            for q in range(4):
                act.wait_ge(xt_done, 4 * (TT - 1) + q + 1)
                act.activation(act32[:, 4 * q:4 * q + 4, P * (TT - 1):P * TT],
                               psum[:, q, :].rearrange("p (k s) -> p k s", k=4), ACT.Copy).then_inc(xt_out, 1)
            act.wait_ge(f_in, 16)
            act.activation(f_hi[:, :, :], f_raw[:, :, :], ACT.Copy).then_inc(f_rounded, 1)
            for k in range(KT):
                act.wait_ge(h_scaled, k + 1)
                act.activation(act_hi[:, k, :], act32[:, k, :], ACT.Copy).then_inc(act_rounded, 1)
            act.wait_ge(f_abs, 1)
            chain(act.activation(f_e[:, :], f_e[:, :], ACT.Exp))
            act.activation(f_e[:, :], f_e[:, :], ACT.Ln, bias=ones[0:NH, :]).then_inc(f_log, 1)

            def round_w(c, w0, r0):
                act.wait_ge(w_in_sem[c % WRING], 16 * (r0 + c // WRING + 1))
                act.wait_ge(w_used, w0 + c + 1)
                act.activation(w_hi[:, c % WRING, :], w_raw[:, c % WRING, :], ACT.Copy).then_inc(w_rounded, 1)

            def take_z(dst, z):
                for t in range(TT):
                    wait_z(act, z, t)
                    act.activation(dst[:, t, :], psum[:, t, :], ACT.Copy).then_inc(z_out, 1)

            def take_heads(dst, n, h, scale):
                act.wait_ge(tr_done, n + 1)
                act.activation(dst[:, h, :], psum[:, 6 + h % 2, :], ACT.Copy, scale=scale).then_inc(tr_out, 1)

            def attention_act(p, g):
                if p < UNITS // 2:
                    for u in (2 * p, 2 * p + 1):
                        n = P * (u % TT + 1)
                        act.wait_ge(s_max, UNITS * g + u + 1)
                        act.wait_ge(pt_done, UNITS * g + u + 1)
                        act.activation(probs[:, u % 2, 0:n], psum[:, 4 + u % 2, 0:n], ACT.Exp,
                                       bias=row_max[:, u % 2:u % 2 + 1], accum_out=row_sum[:, u % 2:u % 2 + 1]).then_inc(s_exp, 1)
                if p > 0:
                    for u in (2 * p - 2, 2 * p - 1):
                        n = P * (u % TT + 1)
                        start = (0, 1, 3, 6)[u % TT] * P
                        act.wait_ge(pt_done, 2 + UNITS * g + u + 1)
                        act.activation(pT[:, u // TT, start:start + n], psum[:, 6 + u % 2, 0:n], ACT.Copy).then_inc(pt_out, 1)

            act.sem_inc(z_out, TT)
            act.sem_inc(tr_out, 2)
            act.sem_inc(s_exp, 2)
            act.sem_inc(pt_out, 2)
            act.sem_inc(o_out, 1)
            act.sem_inc(rv_out, 2)
            act.sem_inc(ot_out, 1)
            with act.Fori(0, GROUPS) as g:
                z0 = FOX_CHUNKS * g
                for c in range(FOX_W):
                    round_w(c, FOX_W * g, FOX_W // WRING * g)
                    if c == 9:
                        take_z(zst, z0)
                    if 13 <= c <= 16:
                        take_heads(kT, 8 * g + c - 13, c - 13, head_cols[:, 1:2])
                    if c == 17:
                        take_z(zst, z0 + 1)
                    if c in (19, 20):
                        for h in (2 * (c - 19), 2 * (c - 19) + 1):
                            take_heads(qT, 8 * g + HG + h, h, head_cols[:, 0:1])
                    if c >= 21:
                        attention_act(2 * (c - 21), g)
                        attention_act(2 * (c - 21) + 1, g)
                attention_act(6, g)
                attention_act(7, g)
                take_z(v_sb, z0 + 2)
                attention_act(8, g)
                act.wait_ge(stage_free, g + 1)
                for h in range(HG):
                    act.wait_ge(pv_done, HG * g + h + 1)
                    act.activation(o_stage[:, h, :], psum[:, 4 + h, :], ACT.Copy).then_inc(o_out, 1)
            with act.Fori(0, GROUPS) as g:
                z0 = Z_RET + RET_CHUNKS * g
                for c in range(RET_W):
                    round_w(c, GROUPS * FOX_W + RET_W * g, GROUPS * FOX_W // WRING + RET_W // WRING * g)
                    if c == 9:
                        take_z(zst, z0)
                    if 13 <= c <= 16:
                        take_heads(qT, 16 + 8 * g + c - 13, c - 13, 1.0)
                    if c == 17:
                        take_z(zst, z0 + 1)
                    if c in (19, 20):
                        act.wait_ge(o_stored, 16 * (GROUPS + g))
                        for h in (2 * (c - 19), 2 * (c - 19) + 1):
                            take_heads(kT, 16 + 8 * g + HG + h, h, 1.0)
                    if c == 25:
                        take_z(v_sb, z0 + 2)
                    if 27 <= c <= 30:
                        h = c - 27
                        act.wait_ge(rv_done, HG * g + h + 1)
                        act.activation(o_sb[:, h, :, :], psum[:, 6 + h % 2, :].rearrange("p (t d) -> p t d", d=HD), ACT.Copy).then_inc(rv_out, 1)
                for t in range(TT):
                    wait_z(act, z0 + 3, t)
                    act.activation(zst[:, t, :], psum[:, t, :], ACT.Exp, scale=-1.0).then_inc(gate_out, 1)
                for n in range(2):
                    tiles = slice(2 * n, 2 * n + 2)
                    act.wait_ge(gate_out, TT * g + 2 * n + 2)
                    act.activation(zst[:, tiles, :], zst[:, tiles, :], ACT.Ln, bias=ones[:, :]).then_inc(gate_log, 1)
                for n in range(2):
                    tiles = slice(2 * n, 2 * n + 2)
                    act.wait_ge(gate_log, 2 * g + n + 1)
                    act.activation(zst[:, tiles, :], zst[:, tiles, :], ACT.Exp, scale=-1.0).then_inc(gate_exp, 1)
                for h in range(HG):
                    act.wait_ge(ot_done, HG * g + h + 1)
                    act.activation(ret_out[:, h, :], psum[:, 4 + h, :], ACT.Copy,
                                   scale=head_cols[:, bass.ds(2 + HG * g + h, 1)]).then_inc(ot_out, 1)
            act.wait_ge(modT_done, 1)
            act.activation(mod_rows_sb[:, :], psum[0:64, 5, 0:P], ACT.Copy).then_inc(modT_out, 1)
            w_first = GROUPS * (FOX_W + RET_W)
            for k in range(KT):
                if k % 4 == 0:
                    round_w(k // 4, w_first, w_first // WRING)
                if k in (0, 5, 10):
                    act.wait_ge(o_in[k // 5], 16)
                if k == 12:
                    act.wait_ge(ot_out, 1 + HG * GROUPS)
                act.activation(act_hi[:, k, :], head_out(k), ACT.Copy).then_inc(act_rounded, 1)
            for c in range(WRING, WC):
                round_w(c, w_first, w_first // WRING)

            def square_x1(n):
                for t in range(TT):
                    act.wait_ge(x1_ready, 2 + TT * n + t + 1)
                    act.wait_ge(x1_square, TT * n + t + 1)
                    act.activation(psum[:, 5, :], x1[:, t, bass.ds(COLS * n, COLS)], ACT.Square,
                                   accum_out=ss2[:, t, bass.ds(n, 1)]).then_inc(x1_square, 1)

            act.sem_inc(x1_square, 1)
            with act.Fori(0, N_OUT - 1) as n:
                for c in range(WC):
                    round_w(c, w_first + WC + WC * n, w_first // WRING + WC // WRING + WC // WRING * n)
                    if c == 2:
                        square_x1(n)
            square_x1(N_OUT - 1)

            def take_logitT(t):
                act.wait_ge(logitT_done, t + 1)
                if t >= 2:
                    act.wait_ge(logit_done, t - 1)
                act.activation(logitT[:, t % 2, :], psum[0:NG + NE, 4, 0:P], ACT.Copy).then_inc(logitT_out, 1)

            def round_m(c, i):
                if i is None:
                    act.wait_ge(m_in[c % RAW], 16)
                else:
                    act.wait_ge(m_in[c % RAW], 32 * i + 16 * (c // RAW + 1))
                    act.wait_ge(m_used, ITEM_PIECES * i + c + 1)
                act.activation(m_hi[:, c % SPL, :], m_raw[:, c % RAW, :], ACT.Copy).then_inc(m_rounded, 1)

            for t in range(TT):
                if t > 0:
                    take_logitT(t - 1)
                for q in range(4):
                    act.wait_ge(h2T_done, 4 * t + q + 1)
                    act.activation(h2T[:, t % 2, 4 * q:4 * q + 4, :], psum[:, q, :].rearrange("p (k s) -> p k s", k=4), ACT.Copy).then_inc(h2T_out, 1)
                round_m(t, None)
            take_logitT(TT - 1)
            act.wait_ge(exp_in, 1)
            act.activation(r_exp[:, :], r_exp[:, :], ACT.Exp).then_inc(coarse_exp, 1)

            def round_x(half, n):
                act.wait_ge(xgT_done, n + 1)
                act.activation(xT[:, 8 * half:8 * half + 8, 0, :], psum[:, 6, :].rearrange("p (k s) -> p k s", s=SLOTS), ACT.Copy).then_inc(xT_rounded, 1)

            act.wait_ge(items_ready, 2)
            items = act.value_load(n_items[0:1, 0:1], min_val=NE, max_val=MAX_ITEMS)
            act.sem_inc(uv_out, 1)
            act.wait_ge(logit_done, TT)
            round_x(0, 0)
            round_x(1, 1)

            def take_y_low(i):
                act.wait_ge(m_used, SPL + ITEM_PIECES * (i + 1))
                act.wait_ge(y_ready, i + 1)
                act.activation(y_low[:, :].rearrange("p (b n) -> p b n", b=4), psum[SLOTS:P, 0:4, :], ACT.Copy).then_inc(y_low_out, 1)

            with act.Fori(0, items) as i:
                for c in range(AHEAD, ITEM_PIECES + AHEAD):
                    round_m(c, i)
                    if c == Y_AFTER:
                        take_y_low(i)
                    if c == UV_AFTER:
                        act.wait_ge(m_used, SPL + ITEM_PIECES * i + 8)
                        act.activation(uv_sb[:, :, :], psum[:, 4:6, :], ACT.Copy).then_inc(uv_out, 1)
                        round_x(0, 2 * i + 2)
                    if c == SILU_AFTER:
                        act.wait_ge(uvT_done, i + 1)
                        act.activation(sig[:, :, :], psum[:, 7, 0:FT * SLOTS].rearrange("p (f s) -> p f s", s=SLOTS), ACT.Exp, scale=-1.0).then_inc(sig_exp, 1)
                        round_x(1, 2 * i + 3)
                    if c == A_AFTER:
                        act.wait_ge(a_ready, i + 1)
                        act.activation(aT[:, :, 0, :], aT32[:, :, :], ACT.Copy).then_inc(a_rounded, 1)
            for t in range(TT):
                act.wait_ge(y_back[t], 16)
                act.activation(fin[:, t, :], y_in[:, t, 0, :], ACT.Copy, scale=gates[:, t, 0:1]).then_inc(y0_scaled, 1)

        @block.vector
        def _(dve):
            chain = Chain(dve, dve_chain, 0)
            dve.sem_inc(ada0_used, 2 * ADA0_RING)
            dve.sem_inc(w_split, WRING)
            dve.sem_inc(ada_used, 2)
            chain(dve.memset(ada_acc[:, :], 0.0))
            dve.wait_ge(c_exp, 1)
            chain(dve.tensor_scalar(c_tmp[:, :], c_tmp[:, :], 1.0, None, ALU.add))
            chain(dve.reciprocal(c_tmp[:, :], c_tmp[:, :]))
            chain(dve.tensor_tensor(c_cols[:, :], c_cols[:, :], c_tmp[:, :], ALU.mult))
            dve.wait_ge(vec_done, 1)
            chain(dve.tensor_copy(vec_cols[:, :], psum[:, 0, 0:P]))
            chain(dve.tensor_copy(head_cols[:, :], psum[:, 1, 0:10]))
            dve.tensor_scalar(head_cols[:, 0:1], head_cols[:, 0:1], HD ** -0.5, None, ALU.mult).then_inc(vec_out, 1)
            with dve.Fori(0, ADA0_GROUPS // 2) as m:
                for a in range(2):
                    for k in range(KT):
                        n = k // 2
                        src = ada0_raw[:, n % ADA0_RING, ADA * (k % 2):ADA * (k % 2 + 1)]
                        if k % 2 == 0:
                            dve.wait_ge(ada0_in[n % ADA0_RING], 64 * m + 32 * a + 16 * (n // ADA0_RING + 1))
                        if k == 0:
                            dve.wait_ge(ada0_sum, 2 * m + a + 1)
                            dve.tensor_scalar(ada0_acc[:, a, :], src, c_cols[:, 0:1], None, ALU.mult).then_inc(ada0_used, 1)
                        else:
                            dve.wait_ge(ada0_used, 2 * ADA0_RING + 2 * KT * m + KT * a + k)
                            dve.scalar_tensor_tensor(ada0_acc[:, a, :], src, c_cols[:, k:k + 1], ada0_acc[:, a, :],
                                                     ALU.mult, ALU.add).then_inc(ada0_used, 1)
                        if k == 3:
                            dve.wait_ge(x_rstd, 2 * m + a + 1)
                            dve.tensor_scalar(x_st[:, a, :], x_st[:, a, :], rstd[:, bass.ds(2 * m + a, 1)], None, ALU.mult).then_inc(x_normed, 1)

            def scale_h(k):
                dve.tensor_scalar(act32[:, k, :], act32[:, k, :], mod_cols[:, 16 + k:17 + k], mod_cols[:, k:k + 1],
                                  ALU.mult, ALU.add).then_inc(h_scaled, 1)

            dve.wait_ge(f_rounded, 1)
            dve.tensor_tensor(f_lo[:, :, :], f_raw[:, :, :], f_hi[:, :, :].bitcast(F32), ALU.subtract).then_inc(f_split, 1)
            dve.wait_ge(xt_out, 4 + 4 * TT)
            dve.wait_ge(ada0_sum, 2 + 3)
            chain(dve.tensor_tensor(mod_cols[:, 0:24].rearrange("p (g j) -> p g j", j=8), psum[:, 4:7, 0:8],
                                    vec_cols[:, 0:24].rearrange("p (g j) -> p g j", j=8), ALU.add))
            chain(dve.scalar_tensor_tensor(mod_cols[:, 16:24], mod_cols[:, 16:24], 1.0, vec_cols[:, 96:104], ALU.add, ALU.mult))
            for k in range(KT // 2):
                scale_h(k)
            dve.wait_ge(ada0_sum, 2 + 4)
            chain(dve.tensor_tensor(mod_cols[:, 24:32], psum[:, 7, 0:8], vec_cols[:, 24:32], ALU.add))
            chain(dve.scalar_tensor_tensor(mod_cols[:, 24:32], mod_cols[:, 24:32], 1.0, vec_cols[:, 104:112], ALU.add, ALU.mult))
            for k in range(KT):
                if k < KT // 2:
                    scale_h(KT // 2 + k)
                dve.wait_ge(act_rounded, k + 1)
                dve.tensor_tensor(act_lo[:, k, :], act32[:, k, :], act_hi[:, k, :].bitcast(F32), ALU.subtract).then_inc(act_split, 1)
            dve.wait_ge(attn_consts_in, 16 * ATTN_CONSTS)
            dve.wait_ge(f_done, 1)
            chain(dve.tensor_scalar(f_y[:, :], psum[0:NH, 4, :], f_bias[:, 0:1], None, ALU.add))
            chain(dve.tensor_scalar(f_e[:, :], f_y[:, :], -1.0, None, ALU.mult))
            dve.tensor_tensor(f_e[:, :], f_e[:, :], f_y[:, :], ALU.min).then_inc(f_abs, 1)
            dve.wait_ge(f_abs, 1)
            chain(dve.tensor_scalar(f_y[:, :], f_y[:, :], 0.0, None, ALU.min))
            dve.wait_ge(f_log, 1)
            chain(dve.tensor_tensor(f_e[:, :], f_e[:, :], f_y[:, :], ALU.subtract))
            dve.wait_ge(consts_set, 3)
            dve.tensor_tensor_scan(neg_cum[:, :], f_ones[:, :], f_e[:, :], 0.0, ALU.mult, ALU.add).then_inc(cum_ready, 1)

            def split_w(c, w0):
                dve.wait_ge(w_rounded, w0 + c + 1)
                dve.tensor_tensor(w_lo[:, c % WRING, :], w_raw[:, c % WRING, :], w_hi[:, c % WRING, :].bitcast(F32),
                                  ALU.subtract).then_inc(w_split, 1)

            def sum_ada(j, a0, r0):
                dve.wait_ge(ada_in[j % 2], r0 + 16 * (j // 2 + 1))
                dve.wait_ge(ada_used, a0 + j + 2)
                dve.scalar_tensor_tensor(ada_acc[:, :], ada_raw[:, j % 2, :], c_cols[:, j % KT:j % KT + 1], ada_acc[:, :],
                                         ALU.mult, ALU.add).then_inc(ada_used, 1)

            def take_ada(group, bank, chain):
                dve.wait_ge(ada_sum, group + 1)
                at8 = bass.ds(32 + 8 * group, 8)
                chain(dve.tensor_reduce(mod_sum[:, :], psum[:, bank:bank + 2, :].rearrange("p b (j q) -> p b j q", q=P).rearrange(
                    "p b j q -> p (b j) q"), AX.X, ALU.add))
                dve.tensor_tensor(mod_cols[:, at8], mod_sum[:, :], vec_cols[:, at8], ALU.add).then_inc(ada_taken, 1)
                chain(dve.memset(ada_acc[:, :], 0.0))
                dve.wait_ge(ada_taken, group + 1)

            def square_heads(z, chain):
                dve.wait_ge(z_out, TT * z + 2 * TT)
                for t in range(TT):
                    chain(dve.tensor_tensor(sq[:, :], zst[:, t, :], zst[:, t, :], ALU.mult))
                    r = dve.tensor_reduce(ssq[:, HG * t:HG * t + HG], sq[:, :].rearrange("p (h d) -> p h d", d=HD), AX.X, ALU.add)
                    if t < TT - 1:
                        chain(r)
                r.then_inc(sq_ready, 1)

            def norm_heads(n):
                dve.wait_ge(rs_ready, n + 1)
                zv = zst[:, :, :].rearrange("p t (h d) -> p (t h) d", d=HD)
                dve.tensor_tensor(zv, zv, rstd[:, :].unsqueeze(2).broadcast_to([P, KT, HD]), ALU.mult).then_inc(z_normed, 1)

            def attention_dve(p, g, chain):
                for u in (2 * p, 2 * p + 1):
                    n = P * (u % TT + 1)
                    dve.wait_ge(s_done, UNITS * g + u + 1)
                    dve.tensor_reduce(row_max[:, u % 2:u % 2 + 1], psum[:, 4 + u % 2, 0:n], AX.X, ALU.max, negate=True).then_inc(s_max, 1)
                for u in (2 * p, 2 * p + 1):
                    n = P * (u % TT + 1)
                    dve.wait_ge(s_exp, 2 + UNITS * g + u + 1)
                    chain(dve.reciprocal(row_inv[:, u % 2:u % 2 + 1], row_sum[:, u % 2:u % 2 + 1]))
                    dve.tensor_scalar(probs[:, u % 2, 0:n], probs[:, u % 2, 0:n], row_inv[:, u % 2:u % 2 + 1], None,
                                      ALU.mult).then_inc(p_normed, 1)

            links = chain.n
            per_body = 2 * (2 * TT - 1) + UNITS + 2 * ADA_GROUPS
            with dve.Fori(0, GROUPS) as g:
                body = Chain(dve, dve_chain, links + per_body * g)
                z0 = FOX_CHUNKS * g
                dve.tensor_copy(head_sel[:, :], one_head[:, bass.ds(HG * P * g, HG * P)]).then_inc(sel_ready, 1)
                j = 0
                for c in range(FOX_W):
                    split_w(c, FOX_W * g)
                    for _ in range(extra_pieces(c)):
                        if j == KT:
                            take_ada(ADA_GROUPS * g, 4, body)
                        sum_ada(j, ADA_BODY * g, 16 * ADA_BODY // 2 * g)
                        j += 1
                    if c in (9, 17):
                        square_heads(z0 + c // 16, body)
                    if c in (10, 18):
                        norm_heads(2 * g + c // 16)
                    if c >= 21:
                        attention_dve(2 * (c - 21), g, body)
                        attention_dve(2 * (c - 21) + 1, g, body)
                attention_dve(6, g, body)
                attention_dve(7, g, body)
                take_ada(ADA_GROUPS * g + 1, 0, body)
                assert body.n == per_body, body.n
            links += per_body * GROUPS

            def rotate(z, part, chain):
                zh = zst[:, :, :].rearrange("p t (h c d) -> p t h c d", h=HG, c=2)
                cos, sin = (rot_tab[:, n, :, :].unsqueeze(2).broadcast_to([P, TT, HG, HD // 2]) for n in range(2))
                z1, z2, r1, r2_ = zh[:, :, :, 0, :], zh[:, :, :, 1, :], rot[:, :, :, 0, :], rot[:, :, :, 1, :]
                if part == 0:
                    dve.wait_ge(z_out, TT * z + 2 * TT)
                    dve.tensor_tensor(r1, z1, cos, ALU.mult)
                    chain(dve.tensor_tensor(r2_, z1, sin, ALU.mult))
                    chain(dve.tensor_tensor(z1, z2, sin, ALU.mult))
                    chain(dve.tensor_tensor(z2, z2, cos, ALU.mult))
                else:
                    chain(dve.tensor_tensor(r1, r1, z1, ALU.subtract))
                    dve.tensor_tensor(r2_, r2_, z2, ALU.add).then_inc(z_normed, 1)

            def decay_scores(u, g):
                h, jt = u // TT, u % TT
                n = S - P * jt
                if jt == 0:
                    dve.wait_ge(decay_in[h % 2], 32 * g + 16 * (h // 2) + 16)
                dve.wait_ge(st_done, UNITS * g + u + 1)
                start = (0, 512, 896, 1152)[jt]
                dve.tensor_tensor(pT[:, h, start:start + n], psum[:, 4 + u % 2, 0:n], decay[:, h % 2, 0:n], ALU.mult).then_inc(st_out, 1)
                if jt == TT - 1:
                    dve.wait_ge(st_out, 2 + UNITS * g + u + 1)
                    dve.sem_inc(decay_used, 1)

            def norm_retention(h, g, chain):
                dve.wait_ge(rv_out, 2 + HG * g + h + 1)
                ov = o_sb[:, h, :, :]
                chain(dve.tensor_tensor(sq[:, :], ov.rearrange("p t d -> p (t d)"), ov.rearrange("p t d -> p (t d)"), ALU.mult))
                cols = slice(TT * h, TT * (h + 1))
                dve.tensor_reduce(ssq[:, cols], sq[:, :].rearrange("p (t d) -> p t d", d=HD), AX.X, ALU.add).then_inc(sq_ready, 1)
                dve.wait_ge(rs_ready, 2 * GROUPS + HG * g + h + 1)
                chain(dve.tensor_tensor(ov, ov, rstd[:, cols].unsqueeze(2).broadcast_to([P, TT, HD]), ALU.mult))

            dve.sem_inc(st_out, 2)
            dve.sem_inc(decay_used, 2)
            per_body = 2 * 4 + 2 * HG + 2 * ADA_GROUPS
            with dve.Fori(0, GROUPS) as g:
                body = Chain(dve, dve_chain, links + per_body * g)
                z0 = Z_RET + RET_CHUNKS * g
                group0 = ADA_GROUPS * (GROUPS + g)
                for c in range(RET_W):
                    split_w(c, GROUPS * FOX_W + RET_W * g)
                    if c == KT:
                        take_ada(group0, 4, body)
                    sum_ada(c, ADA_BODY * (GROUPS + g), 16 * ADA_BODY // 2 * (GROUPS + g))
                    if c in (9, 10, 17, 18):
                        rotate(z0 + c // 16, (c - 1) % 2, body)
                    if 21 <= c <= 24:
                        for u in range(4 * (c - 21), 4 * (c - 21) + 4):
                            decay_scores(u, g)
                    if 28 <= c <= 31:
                        norm_retention(c - 28, g, body)
                for t in range(TT):
                    dve.wait_ge(gate_out, TT * g + t + 1)
                    ov = o_sb[:, :, t, :]
                    dve.tensor_tensor(ov, ov, psum[:, t, :].rearrange("p (h d) -> p h d", h=HG), ALU.mult).then_inc(z_out, 1)
                take_ada(group0 + 1, 0, body)
                dve.wait_ge(z_out, TT * (z0 + 3) + 2 * TT)
                for n in range(2):
                    tiles = slice(2 * n, 2 * n + 2)
                    dve.wait_ge(gate_exp, 2 * g + n + 1)
                    ov = o_sb[:, :, tiles, :].rearrange("p h t d -> p t h d")
                    dve.tensor_tensor(ov, ov, zst[:, tiles, :].rearrange("p t (h d) -> p t h d", h=HG), ALU.mult).then_inc(o_gated, 1)
                assert body.n == per_body, body.n
            links += per_body * GROUPS
            chain = Chain(dve, dve_chain, links)
            dve.wait_ge(ada_taken, 2 * ADA_GROUPS * GROUPS)
            dve.scalar_tensor_tensor(mod_cols[:, 64:80], mod_cols[:, 64:80], 1.0, vec_cols[:, 112:128], ALU.add, ALU.mult).then_inc(mod_ready, 1)
            dve.sem_inc(mix_out, TT)
            dve.sem_inc(x1_ready, 2)
            w_first = GROUPS * (FOX_W + RET_W)
            for k in range(KT):
                if k % 4 == 0:
                    split_w(k // 4, w_first)
                dve.wait_ge(act_rounded, KT + k + 1)
                dve.tensor_tensor(act_lo[:, k, :], head_out(k), act_hi[:, k, :].bitcast(F32), ALU.subtract).then_inc(act_split, 1)
            for c in range(WRING, WC):
                split_w(c, w_first)

            def add_mix(n):
                dve.wait_ge(g1_in, 16)
                dve.wait_ge(x_again, 16 * TT)
                cols = bass.ds(COLS * n, COLS)
                for t in range(TT):
                    wait_z(dve, Z_OUT + n, t)
                    dve.wait_ge(x1_ready, TT * n + t + 1)
                    dve.tensor_tensor(psum[:, 6 + t % 2, :], psum[:, t, :], g1_row[:, cols], ALU.mult).then_inc(mix_out, 1)
                    dve.wait_ge(mix_out, TT + TT * n + t + 1)
                    dve.tensor_tensor(x1[:, t, cols], x1[:, t, cols], psum[:, 6 + t % 2, :], ALU.add).then_inc(x1_ready, 1)

            with dve.Fori(0, N_OUT - 1) as n:
                for c in range(WC):
                    split_w(c, w_first + WC + WC * n)
                    if c == 2:
                        add_mix(n)
            add_mix(N_OUT - 1)
            dve.sem_inc(m_split, 4)
            dve.wait_ge(x1_square, 1 + TT * N_OUT)
            dve.tensor_reduce(ms2[:, :], ss2[:, :, :], AX.X, ALU.add).then_inc(ms2_ready, 1)
            dve.wait_ge(r2_ready, 1)
            dve.wait_ge(row2_in, 32)
            for t in range(TT):
                if t == 3:
                    dve.wait_ge(h2_stored[0], 16)
                    dve.wait_ge(h2T_done, 4)
                h2v = h2[:, t % 3, :].rearrange("p (k q) -> p q k", k=KT)
                nat = "p (q k) -> p q k"
                chain(dve.scalar_tensor_tensor(h2v, x1[:, t, :].rearrange(nat, k=KT), r2[:, t:t + 1], scale2[:, :].rearrange(nat, k=KT),
                                               ALU.mult, ALU.mult))
                dve.tensor_tensor(h2v, h2v, shift2[:, :].rearrange(nat, k=KT), ALU.add).then_inc(h2_ready, 1)
            dve.wait_ge(h2_ready, TT)
            dve.sem_inc(m_split, 2)

            def split_m(c, i):
                dve.wait_ge(m_rounded, ITEM_PIECES * i + c + 1)
                dve.tensor_tensor(m_lo[:, c % SPL, :], m_raw[:, c % RAW, :], m_hi[:, c % SPL, :].bitcast(F32),
                                  ALU.subtract).then_inc(m_split, 1)

            dve.wait_ge(route_in, 16 * ROUTE_CONSTS)
            chain(dve.memset(coarse8[:, :], -BIG))
            for t in range(TT):
                if t < AHEAD - 1:
                    split_m(t, 0)
                dve.wait_ge(logit_done, t + 1)
                dve.tensor_tensor(logit[:, t, :], psum[:, 6 + t % 2, 0:NG + NE], route_b[:, :], ALU.add).then_inc(logit_taken, 1)
                dve.wait_ge(logit_taken, t + 1)
                chain(dve.tensor_copy(coarse8[:, 0:NG], logit[:, t, 0:NG]))
                chain(dve.max(top8[:, 0, :], coarse8[:, :]))
                chain(dve.max_index(idx8[:, 0, :], top8[:, 0, :], coarse8[:, :]))
                chain(dve.tensor_scalar(r_exp[:, NG * t:NG * t + NG], logit[:, t, 0:NG], top8[:, 0, 0:1], None, ALU.subtract))
                chain(dve.tensor_copy(small[:, 0:1], idx8[:, 0, 0:1]))
                chain(dve.tensor_scalar(small[:, 4:8], iota[:, 0:NG], small[:, 0:1], -1.0, ALU.is_equal, ALU.add))
                chain(dve.tensor_scalar(small[:, 8:12], small[:, 4:8], BIG, None, ALU.mult))
                chain(dve.tensor_tensor(fine[:, :].rearrange("p (g e) -> p g e", g=NG),
                                        logit[:, t, NG:].rearrange("p (g e) -> p g e", g=NG),
                                        small[:, 8:12].unsqueeze(2).broadcast_to([P, NG, EPG]), ALU.add))
                chain(dve.max(top8[:, 1, :], fine[:, :]))
                chain(dve.max_index(idx8[:, 1, :], top8[:, 1, :], fine[:, :]))
                chain(dve.tensor_copy(pick[:, t, :], idx8[:, 1, 0:2]))
                chain(dve.tensor_tensor(r_exp[:, KT + t:KT + t + 1], top8[:, 1, 1:2], top8[:, 1, 0:1], ALU.subtract))
                for k in range(2):
                    chain(dve.tensor_scalar(hot[:, t, k, :], iota[:, 0:NE], pick[:, t, k:k + 1], None, ALU.is_equal))
                dve.tensor_tensor(member[:, t, :], hot[:, t, 0, :], hot[:, t, 1, :], ALU.add).then_inc(member_ready, 1)
            dve.sem_inc(exp_in, 1)
            dve.wait_ge(coarse_exp, 1)
            e1 = r_exp[:, KT:KT + TT]
            chain(dve.tensor_reduce(small[:, 0:TT], r_exp[:, 0:KT].rearrange("p (t g) -> p t g", g=NG), AX.X, ALU.add))
            chain(dve.scalar_tensor_tensor(small[:, 4:8], e1, 1.0, small[:, 0:TT], ALU.add, ALU.mult))
            chain(dve.reciprocal(small[:, 8:12], small[:, 4:8]))
            chain(dve.tensor_copy(gates[:, :, 0], small[:, 8:12]))
            chain(dve.tensor_tensor(gates[:, :, 1], small[:, 8:12], e1, ALU.mult))
            dve.wait_ge(rank_done, 1)
            chain(dve.tensor_scalar(count_i[:, :], psum[:, 5, TT * NE:(TT + 1) * NE], float(SLOTS - 1), None, ALU.add))
            chain(dve.tensor_scalar(count_i[:, :], count_i[:, :], 6, None, ALU.logical_shift_right))
            chain(dve.tensor_scalar(over[:, :], count_i[:, :], -1.0, 0.0, ALU.add, ALU.max))
            chain(dve.tensor_tensor_scan(over_end[:, :], ones2[:, 0:NE], over[:, :], 0.0, ALU.mult, ALU.add))
            dve.tensor_scalar(n_items[0:1, 0:1], over_end[0:1, NE - 1:NE], float(NE), None, ALU.add).then_inc(items_ready, 1)
            chain(dve.tensor_tensor(over_from[:, :], over_end[:, :], over[:, :], ALU.subtract))
            hv = hot[:, :, :, :].rearrange("p t k e -> p (t k) e")
            w4 = wide[:, :, :].rearrange("p (t k) e -> p t k e", k=2)
            chain(dve.tensor_tensor(w4, hot[:, :, :, :], psum[:, 5, 0:TT * NE].rearrange("p (t e) -> p t e", e=NE).unsqueeze(2).broadcast_to([P, TT, 2, NE]), ALU.mult))
            chain(dve.tensor_reduce(per[:, 0, :], wide[:, :, :], AX.X, ALU.add))
            chain(dve.tensor_tensor(wide[:, :, :], hv, over_from[:, :].unsqueeze(1).broadcast_to([P, 2 * TT, NE]), ALU.mult))
            chain(dve.tensor_reduce(per[:, 1, :], wide[:, :, :], AX.X, ALU.add))
            e_pick = pick[:, :, :].rearrange("p t k -> p (t k)")
            chain(dve.tensor_copy(per_i[:, 0, :], per[:, 0, :]))
            chain(dve.tensor_scalar(per_i[:, 1, :], per_i[:, 0, :], 6, None, ALU.logical_shift_right))
            chain(dve.tensor_copy(per[:, 2, :], per_i[:, 1, :]))
            chain(dve.scalar_tensor_tensor(per[:, 3, :], per[:, 2, :], -float(SLOTS), per[:, 0, :], ALU.mult, ALU.add))
            chain(dve.tensor_scalar(per[:, 4, :], per[:, 2, :], 0.0, None, ALU.is_equal))
            chain(dve.scalar_tensor_tensor(per[:, 5, :], per[:, 1, :], float(NE - 1), per[:, 2, :], ALU.add, ALU.add))
            chain(dve.tensor_tensor(per[:, 6, :], e_pick, per[:, 5, :], ALU.subtract))
            chain(dve.tensor_tensor(per[:, 6, :], per[:, 6, :], per[:, 4, :], ALU.mult))
            chain(dve.tensor_tensor(per[:, 6, :], per[:, 6, :], per[:, 5, :], ALU.add))
            iota_n = iota[:, :].unsqueeze(1).broadcast_to([P, 2 * TT, SLOTS])
            chain(dve.tensor_tensor(slot_hot[:, :, :], iota_n, per[:, 3, :].unsqueeze(2).broadcast_to([P, 2 * TT, SLOTS]), ALU.is_equal))
            chain(dve.tensor_tensor(column_hot[:, :, :], iota_n[:, :, 0:TABLE],
                                    per[:, 6, :].unsqueeze(2).broadcast_to([P, 2 * TT, TABLE]), ALU.is_equal))
            for n in range(2):
                dve.tensor_tensor(entry_hot[:, :, n, :], column_hot[:, :, :], entry[:, n, :].unsqueeze(2).broadcast_to([P, 2 * TT, TABLE]),
                                  ALU.mult).then_inc(entries_hot, 1)
            extra = MAX_ITEMS - NE
            chain(dve.tensor_tensor(which_o[:, :, :], over_end[0:1, :].unsqueeze(1).broadcast_to([1, extra, NE]),
                                    iota[0:1, 0:extra].unsqueeze(2).broadcast_to([1, extra, NE]), ALU.is_le))
            chain(dve.tensor_reduce(extra_f[:, :], which_o[:, :, :], AX.X, ALU.add))
            dve.tensor_scalar(extra_e[:, :], extra_f[:, :], float(NE - 1), None, ALU.min).then_inc(items_ready, 1)
            split_m(AHEAD - 1, 0)
            dve.wait_ge(entries_placed, 1)
            dve.tensor_scalar(table[:, :, :], psum[0:SLOTS, 6, 0:2 * TABLE].rearrange("s (c i) -> s c i", c=2), float(NOWHERE), None,
                              ALU.add).then_inc(table_ready, 1)

            dve.wait_ge(items_ready, 2)
            items = dve.value_load(n_items[0:1, 0:1], min_val=NE, max_val=MAX_ITEMS)
            dve.sem_inc(y_ready, 1)

            def split_x(half, n):
                dve.wait_ge(xT_rounded, n + 1)
                ks = slice(8 * half, 8 * half + 8)
                dve.tensor_tensor(xT[:, ks, 1, :], psum[:, 6, :].rearrange("p (k s) -> p k s", s=SLOTS), xT[:, ks, 0, :].bitcast(F32),
                                  ALU.subtract).then_inc(xT_split, 1)

            split_x(0, 0)
            split_x(1, 1)
            links += chain.n

            def add_y(i):
                dve.wait_ge(y_low_out, i + 1)
                dve.wait_ge(y_free, i + 1)
                dve.tensor_tensor(y_sb[:, :].rearrange("p (b n) -> p b n", b=4), psum[0:SLOTS, 0:4, :],
                                  y_low[:, :].rearrange("p (b n) -> p b n", b=4), ALU.add).then_inc(y_ready, 1)

            with dve.Fori(0, items) as i:
                body = Chain(dve, dve_chain, links + 3 * i)
                for c in range(AHEAD, ITEM_PIECES + AHEAD):
                    split_m(c, i)
                    if c == Y_AFTER:
                        add_y(i)
                    if c == UV_AFTER:
                        split_x(0, 2 * i + 2)
                    if c == SILU_AFTER:
                        dve.wait_ge(sig_exp, i + 1)
                        u_v = psum[:, 7, :].rearrange("p (w f s) -> p w f s", w=2, s=SLOTS)
                        body(dve.tensor_scalar(sig[:, :, :], sig[:, :, :], 1.0, None, ALU.add))
                        body(dve.reciprocal(sig[:, :, :], sig[:, :, :]))
                        body(dve.tensor_tensor(sig[:, :, :], sig[:, :, :], u_v[:, 0, :, :], ALU.mult))
                        dve.tensor_tensor(aT32[:, :, :], sig[:, :, :], u_v[:, 1, :, :], ALU.mult).then_inc(a_ready, 1)
                        split_x(1, 2 * i + 3)
                    if c == SILU_AFTER:
                        dve.wait_ge(a_rounded, i + 1)
                        dve.tensor_tensor(aT[:, :, 1, :], aT32[:, :, :], aT[:, :, 0, :].bitcast(F32), ALU.subtract).then_inc(a_split, 1)
            done = Chain(dve, dve_chain, links + 3 * items)
            dve.wait_ge(g2_in, 16)
            for t in range(TT):
                f = fin[:, t, :]
                dve.wait_ge(y0_scaled, t + 1)
                done(dve.scalar_tensor_tensor(f, y_in[:, t, 1, :], gates[:, t, 1:2], f, ALU.mult, ALU.add))
                done(dve.tensor_tensor(f, f, g2_row[:, :], ALU.mult))
                dve.tensor_tensor(f, f, x1[:, t, :], ALU.add).then_inc(fin_ready, 1)

        @block.tensor
        def _(pe):
            mm = pe.matmul
            pe.wait_ge(consts_in, 16 * HEAD_CONSTS)
            mm(psum[:, 0, 0:P], vec_rows[:, :], ident[:, :], is_transpose=True, start=True, stop=True)
            mm(psum[:, 1, 0:10], head_rows[:, :], ident[0:10, 0:10], is_transpose=True, start=True, stop=True).then_inc(vec_done, 1)
            pe.wait_ge(vec_out, 1)
            pe.wait_ge(consts_set, 3)
            pe.sem_inc(ada0_sum, 2)
            with pe.Fori(0, ADA0_GROUPS // 2) as m2:
                for a in range(2):
                    pe.wait_ge(x_normed, 2 * m2 + a + 1)
                    for q in range(4):
                        pe.wait_ge(xt_out, 8 * m2 + 4 * a + q + 1)
                        for j in range(4):
                            m = pe.transpose(psum[:, q, P * j:P * (j + 1)], x_st[:, a, P * (4 * q + j):P * (4 * q + j + 1)], ident[:, :])
                        m.then_inc(xt_done, 1)
                    pe.wait_ge(ada0_used, 2 * ADA0_RING + 2 * KT * m2 + KT * (a + 1))
                    for j in range(8):
                        m = mm(psum[:, bass.ds(4 + 2 * m2 + a, 1), j:j + 1], ada0_acc[:, a, P * j:P * (j + 1)], ones[:, :], start=True, stop=True)
                    m.then_inc(ada0_sum, 1)
            pe.wait_ge(f_split, 1)
            for k in range(KT):
                pe.wait_ge(act_split, k + 1)
                for n, (wf, act_part) in enumerate(((f_hi, act_hi), (f_lo, act_hi), (f_hi, act_lo))):
                    m = mm(psum[0:NH, 4, :], wf[:, k, :], act_part[:, k, :], start=k == 0 and n == 0, stop=k == KT - 1 and n == 2)
            m.then_inc(f_done, 1)

            def project(k, z, w0, c, free):
                if k % 2 == 0:
                    pe.wait_ge(w_split, WRING + w0 + c + 1)
                half = slice(COLS * (k % 2), COLS * (k % 2 + 1))
                wh, wl = w_hi[:, c % WRING, half], w_lo[:, c % WRING, half]
                for t in range(TT):
                    if k == 0:
                        free(t)
                    tok = slice(P * t, P * (t + 1))
                    mm(psum[:, t, :], act_hi[:, k, tok], wh, start=k == 0, stop=False)
                    mm(psum[:, t, :], act_hi[:, k, tok], wl, start=False, stop=False)
                    m = mm(psum[:, t, :], act_lo[:, k, tok], wh, start=False, stop=k == KT - 1)
                    if k == KT - 1 and t < TT - 1:
                        m.then_inc(z_done, 1)
                if k % 2:
                    m.then_inc(w_used, 1)

            def transpose_heads(n, h, src):
                pe.wait_ge(tr_out, n + 1)
                for t in range(TT):
                    m = pe.transpose(psum[:, 6 + h % 2, P * t:P * (t + 1)], src(t), ident[:, :])
                m.then_inc(tr_done, 1)

            def turn_ada(group, bank):
                pe.wait_ge(ada_used, 2 + KT * (group + 1))
                for j in range(ADA // P):
                    m = pe.transpose(psum[:, bank + j // 4, P * (j % 4):P * (j % 4 + 1)], ada_acc[:, P * j:P * (j + 1)], ident[:, :])
                m.then_inc(ada_sum, 1)

            def attention_scores(p, g):
                for u in (2 * p, 2 * p + 1):
                    h, i = u // TT, u % TT
                    n = P * (i + 1)
                    pe.wait_ge(s_exp, UNITS * g + u + 1)
                    o = psum[:, 4 + u % 2, 0:n]
                    mm(o, qT[:, h, P * i:P * (i + 1)], kT[:, h, 0:n], start=True, stop=False)
                    mm(o, head_sel[:, P * h:P * (h + 1)], neg_cum[:, 0:n], start=False, stop=False)
                    mm(psum[:, 4 + u % 2, P * i:n], ident[:, :], causal[:, :], start=False, stop=True).then_inc(s_done, 1)

            def attention_transpose(p, g):
                for u in (2 * p, 2 * p + 1):
                    pe.wait_ge(p_normed, UNITS * g + u + 1)
                    pe.wait_ge(pt_out, UNITS * g + u + 1)
                    for j in range(u % TT + 1):
                        m = pe.transpose(psum[:, 6 + u % 2, P * j:P * (j + 1)], probs[:, u % 2, P * j:P * (j + 1)], ident[:, :])
                    m.then_inc(pt_done, 1)

            pe.wait_ge(cum_ready, 1)
            pe.sem_inc(w_used, WRING)
            pe.sem_inc(pt_done, 2)
            with pe.Fori(0, GROUPS) as g:
                for c in range(FOX_W):
                    z = FOX_CHUNKS * g + c // WC

                    def free(t):
                        pe.wait_ge(z_out, TT * z + t + 1)

                    for k in (2 * (c % WC), 2 * (c % WC) + 1):
                        step = KT * (c // WC) + k
                        project(k, z, FOX_W * g, c, free)
                        if step == 23:
                            pe.wait_ge(o_out, 1 + HG * g)
                            turn_ada(ADA_GROUPS * g, 4)
                        if 24 <= step <= 30 and step % 2 == 0:
                            h = (step - 24) // 2
                            if h == 0:
                                pe.wait_ge(z_normed, 2 * g + 1)
                            transpose_heads(8 * g + h, h, lambda t: zst[:, t, HD * h:HD * (h + 1)])
                        if 36 <= step <= 39:
                            h = step - 36
                            if h == 0:
                                pe.wait_ge(z_normed, 2 * g + 2)
                            transpose_heads(8 * g + HG + h, h, lambda t: zst[:, t, HD * h:HD * (h + 1)])
                        if step == 39:
                            pe.wait_ge(tr_out, 2 + 8 * g + 8)
                        if step >= 40:
                            p = step - 40
                            if p == 0:
                                pe.wait_ge(sel_ready, g + 1)
                            attention_scores(p, g)
                            if p > 0:
                                attention_transpose(p - 1, g)
                attention_transpose(UNITS // 2 - 1, g)
                pe.wait_ge(z_out, TT + TT * FOX_CHUNKS * (g + 1))
                pe.wait_ge(pt_out, 2 + UNITS * (g + 1))
                turn_ada(ADA_GROUPS * g + 1, 0)
                for h in range(HG):
                    for i in range(TT):
                        start = (0, 1, 3, 6)[i]
                        for j in range(i + 1):
                            m = mm(psum[:, 4 + h, P * i:P * (i + 1)], v_sb[:, j, HD * h:HD * (h + 1)],
                                   pT[:, h, P * (start + j):P * (start + j + 1)], start=j == 0, stop=j == i)
                    m.then_inc(pv_done, 1)
                pe.wait_ge(ada_taken, ADA_GROUPS * (g + 1))
            pe.wait_ge(o_out, 1 + HG * GROUPS)
            with pe.Fori(0, GROUPS) as g:
                for c in range(RET_W):
                    z = Z_RET + RET_CHUNKS * g + c // WC

                    def free(t):
                        pe.wait_ge(z_out, TT * z + t + 1)

                    for k in (2 * (c % WC), 2 * (c % WC) + 1):
                        step = KT * (c // WC) + k
                        project(k, z, GROUPS * FOX_W + RET_W * g, c, free)
                        if 24 <= step <= 30 and step % 2 == 0:
                            h = (step - 24) // 2
                            if h == 0:
                                pe.wait_ge(z_normed, 4 + 2 * g + 1)
                                pe.wait_ge(ot_out, HG * g + 1)
                            transpose_heads(16 + 8 * g + h, h, lambda t: rot[:, t, h, :, :].rearrange("p c d -> p (c d)"))
                        if step == 31:
                            turn_ada(ADA_GROUPS * (GROUPS + g), 4)
                        if 36 <= step <= 39:
                            h = step - 36
                            if h == 0:
                                pe.wait_ge(z_normed, 4 + 2 * g + 2)
                            transpose_heads(16 + 8 * g + HG + h, h, lambda t: rot[:, t, h, :, :].rearrange("p c d -> p (c d)"))
                        if step == 39:
                            pe.wait_ge(tr_out, 2 + 16 + 8 * g + 8)
                        if 40 <= step <= 47:
                            for u in (2 * (step - 40), 2 * (step - 40) + 1):
                                h, j = u // TT, u % TT
                                pe.wait_ge(st_out, UNITS * g + u + 1)
                                mm(psum[:, 4 + u % 2, 0:S - P * j], kT[:, h, P * j:P * (j + 1)], qT[:, h, P * j:S],
                                   start=True, stop=True).then_inc(st_done, 1)
                        if 52 <= step <= 58 and step % 2 == 0:
                            h = (step - 52) // 2
                            if h == 0:
                                pe.wait_ge(z_out, TT + TT * (Z_RET + RET_CHUNKS * g + 3))
                            pe.wait_ge(st_out, 2 + UNITS * g + TT * (h + 1))
                            pe.wait_ge(rv_out, HG * g + h + 1)
                            for i in range(TT):
                                for j in range(i + 1):
                                    start = (0, 512, 896, 1152)[j] + P * (i - j)
                                    m = mm(psum[:, 6 + h % 2, P * i:P * (i + 1)], pT[:, h, start:start + P],
                                           v_sb[:, j, HD * h:HD * (h + 1)], start=j == 0, stop=j == i)
                            m.then_inc(rv_done, 1)
                pe.wait_ge(z_out, TT + TT * (Z_RET + RET_CHUNKS * g + 3) + 2)
                turn_ada(ADA_GROUPS * (GROUPS + g) + 1, 0)
                pe.wait_ge(rv_out, 2 + HG * (g + 1))
                for n in range(2):
                    pe.wait_ge(o_gated, 2 * g + n + 1)
                    for h in range(HG):
                        for t in (2 * n, 2 * n + 1):
                            m = pe.transpose(psum[:, 4 + h, P * t:P * (t + 1)], o_sb[:, h, t, :], ident[:, :])
                        if n == 1:
                            m.then_inc(ot_done, 1)
            pe.wait_ge(mod_ready, 1)
            pe.wait_ge(ot_out, 1 + HG * GROUPS)
            pe.transpose(psum[0:64, 5, 0:P], mod_cols[:, 32:96], ident[:, :]).then_inc(modT_done, 1)
            pe.wait_ge(z_out, TT + TT * Z_OUT)
            w_first = GROUPS * (FOX_W + RET_W)
            with pe.Fori(0, N_OUT // 2) as m2:
                for c in range(2 * WC):
                    n = 2 * m2 + c // WC

                    def free(t):
                        pe.wait_ge(mix_out, TT * n + t + 1)

                    for k in (2 * (c % WC), 2 * (c % WC) + 1):
                        pe.wait_ge(act_split, KT + k + 1)
                        project(k, Z_OUT + n, w_first + 2 * WC * m2, c, free)
            pe.wait_ge(mix_out, TT + TT * N_OUT)

            def logits_back(t):
                pe.wait_ge(logitT_out, t + 1)
                if t >= 2:
                    pe.wait_ge(logit_taken, t - 1)
                pe.transpose(psum[:, 6 + t % 2, 0:NG + NE], logitT[:, t % 2, :], ident[0:NG + NE, 0:NG + NE]).then_inc(logit_done, 1)

            def ranks(t):
                pe.wait_ge(member_ready, t + 1)
                for t2 in range(t + 1):
                    mm(psum[:, 5, NE * t:NE * (t + 1)], strict[:, :] if t2 == t else ones2[:, :], member[:, t2, :],
                       start=t2 == 0, stop=t2 == t)

            pe.wait_ge(route_in, 16 * ROUTE_CONSTS)
            pe.wait_ge(consts_set, 4)
            for t in range(TT):
                pe.wait_ge(h2_ready, t + 1)
                for q in range(4):
                    if t > 0:
                        pe.wait_ge(h2T_out, 4 * (t - 1) + q + 1)
                    for j in range(4):
                        m = pe.transpose(psum[:, q, P * j:P * (j + 1)], h2[:, t % 3, P * (4 * q + j):P * (4 * q + j + 1)], ident[:, :])
                    m.then_inc(h2T_done, 1)
                if t > 0:
                    logits_back(t - 1)
                for k in range(KT):
                    if k % 4 == 0:
                        pe.wait_ge(h2T_out, 4 * t + k // 4 + 1)
                    m = mm(psum[0:NG + NE, 4, 0:P], route_w[:, k, :], h2T[:, t % 2, k, :], start=k == 0, stop=k == KT - 1)
                m.then_inc(logitT_done, 1)
                if t > 1:
                    ranks(t - 2)
            logits_back(TT - 1)
            ranks(TT - 2)
            ranks(TT - 1)
            for t in range(TT):
                m = mm(psum[:, 5, NE * TT:NE * (TT + 1)], ones2[:, :], member[:, t, :], start=t == 0, stop=t == TT - 1)
            m.then_inc(rank_done, 1)
            pe.wait_ge(logit_taken, TT)
            pe.wait_ge(entries_hot, 2)
            for n in range(2 * TT):
                m = mm(psum[0:SLOTS, 6, 0:2 * TABLE], slot_hot[:, n, :], entry_hot[:, n, :, :].rearrange("p c i -> p (c i)"),
                       start=n == 0, stop=n == 2 * TT - 1)
            m.then_inc(entries_placed, 1)

            def transpose_rows(half, n):
                if n is not None:
                    hold(pe, xT_split, n)
                for j in range(8):
                    k = 8 * half + j
                    m = pe.transpose(psum[:, 6, SLOTS * j:SLOTS * (j + 1)], xg[:, P * k:P * (k + 1)], ident[0:SLOTS, 0:SLOTS])
                m.then_inc(xgT_done, 1)

            pe.wait_ge(items_ready, 2)
            items = pe.value_load(n_items[0:1, 0:1], min_val=NE, max_val=MAX_ITEMS)
            pe.sem_inc(m_used, SPL)
            pe.wait_ge(pair_in, 16)
            pe.wait_ge(xg_in, 16)
            pe.wait_ge(table_ready, 1)
            transpose_rows(0, None)
            transpose_rows(1, 1)
            with pe.Fori(0, items) as i:
                pe.wait_ge(xT_split, 2 * i + 2)
                pe.wait_ge(uv_out, i + 1)
                for c in range(8):
                    pe.wait_ge(m_split, RAW + ITEM_PIECES * i + c + 1)
                    for j in range(4):
                        k = 4 * (c // 2) + j
                        x_both = xT[:, k, :, :].rearrange("p c s -> p (c s)")
                        for part in (m_hi, m_lo):
                            m = mm(psum[:, 4 + c % 2, :], x_both, part[:, c % SPL, DE * j:DE * (j + 1)],
                                   start=k == 0 and part is m_hi, stop=k == KT - 1 and part is m_lo)
                    m.then_inc(m_used, 1)
                pe.wait_ge(xg_in, 16 * i + 32)
                transpose_rows(0, 2 * i + 2)
                pe.wait_ge(uv_out, i + 2)
                for w in range(2):
                    for f in range(FT):
                        m = mm(psum[:, 7, SLOTS * (FT * w + f):SLOTS * (FT * w + f + 1)], uv_sb[:, w, P * f:P * (f + 1)], pair[:, :],
                               start=True, stop=True)
                m.then_inc(uvT_done, 1)
                transpose_rows(1, 2 * i + 3)
                pe.wait_ge(a_split, i + 1)
                pe.wait_ge(y_ready, i + 1)
                for c in range(8, ITEM_PIECES):
                    f = c - 8
                    pe.wait_ge(m_split, RAW + ITEM_PIECES * i + c + 1)
                    a_both = aT[:, f, :, :].rearrange("p c s -> p (c s)")
                    for part in (m_hi, m_lo):
                        for b in range(4):
                            m = mm(psum[:, b, :], a_both, part[:, c % SPL, DE * b:DE * (b + 1)],
                                   start=f == 0 and part is m_hi, stop=f == FT - 1 and part is m_lo)
                    m.then_inc(m_used, 1)


_INS = ["x", "c", "w_ada", "b_ada", "norm1_w", "w_in", "forget_bias", "q_norm_w", "k_norm_w", "ret_norm_w", "w_out",
        "norm2_w", "w_coarse", "b_coarse", "w_fine", "b_fine", "w1", "w3", "w2"]


def kernel(**inputs):
    import concourse.bacc as bacc
    from concourse.bass_utils import run_bass_kernel_spmd

    nc = bacc.Bacc("TRN2", target_bir_lowering=False, num_devices=1)
    arrays, A = {}, {}
    for name, a in [(n, inputs[n]) for n in _INS] + list(constants().items()):
        a = np.ascontiguousarray(a)
        arrays[f"in_{name}"] = a
        A[name] = nc.dram_tensor(f"in_{name}", a.shape, mybir.dt.from_np(a.dtype), kind="ExternalInput").ap()
    out = nc.dram_tensor("out", (1, S, D), F32, kind="ExternalOutput").ap()
    hybrid_block(nc, A, out)
    r = run_bass_kernel_spmd(nc, [arrays], core_ids=[0])
    return r.results[0]["out"]
```
